# Optimizing a Trainium2 kernel written in Bass

```python
import jax, jax.numpy as jnp
from jax import lax
import numpy as np

D_MODEL = 1024
BATCH = 1
SEQ = 128
DEPTH = 4
DEC_BATCH = 1
DEC_SEQ = 512
PAST_LEN = 128

GRID_W = 64
N_MIXERS = 4
N_MOD = 6
D_FF = 4 * D_MODEL
EPS = 1e-6
FFT_GROUPS = 8
RWKV_HS = 64
RWKV_H = D_MODEL // RWKV_HS
LORA_W = 64
LORA_A = 64
LORA_G = 128
GN_EPS = 64e-5
MLA_H = 8
D_NOPE = 128
D_ROPE = 64
D_V = 128
KV_RANK = 256
Q_RANK = 384
ROPE_BASE = 10000.0
MLA_SCALE = (D_NOPE + D_ROPE) ** -0.5
N_FFT_LAYERS = (DEPTH + 3) // 4
N_CONV_LAYERS = (DEPTH + 2) // 4
N_RWKV_LAYERS = (DEPTH + 1) // 4
N_MLA_LAYERS = DEPTH // 4

kernel_name = "hybrid_fourier_conv_rwkv7_mla_diffusion_step"

def rmsnorm(x, g):
    xf = x.astype(jnp.float32)
    y = xf * lax.rsqrt(jnp.mean(xf * xf, axis=-1, keepdims=True) + EPS)
    return (y * g).astype(x.dtype)

def modulation(cvec, w, b):
    m = jax.nn.silu(cvec) @ w + b
    return jnp.split(m[:, None, :], N_MOD, axis=-1)

def shift_neighbours(x):
    xp = jnp.pad(x, ((0, 0), (1, 1), (0, 0)))
    return xp[:, :-2], xp[:, 2:]

def fourier_mix(x, w_out):
    b, n, d = x.shape
    xg = x.astype(jnp.float32).reshape(b, n, FFT_GROUPS, d // FFT_GROUPS)
    f = jnp.fft.fft2(xg, axes=(1, 3), norm="ortho").real
    return f.reshape(b, n, d).astype(x.dtype) @ w_out

def short_conv_mix(x, w_in, w_conv, w_out):
    bg, cg, u = jnp.split(x @ w_in, 3, axis=-1)
    z = cg * u
    z_prev, z_next = shift_neighbours(z)
    conv = z_prev * w_conv[0] + z * w_conv[1] + z_next * w_conv[2]
    return (bg * conv) @ w_out

def wkv7_scan(s0, r, w, k, v, kk, a, reverse):
    def step(s, inp):
        rt, wt, kt, vt, kkt, at = inp
        sa = jnp.einsum('bhvk,bhk->bhv', s, -kkt)
        s = s * wt[:, :, None, :] + sa[..., None] * (kkt * at)[:, :, None, :] + vt[..., None] * kt[:, :, None, :]
        return s, jnp.einsum('bhvk,bhk->bhv', s, rt)
    xs = tuple(jnp.moveaxis(t, 1, 0) for t in (r, w, k, v, kk, a))
    s_fin, ys = lax.scan(step, s0, xs, reverse=reverse)
    return s_fin, jnp.moveaxis(ys, 0, 1)

def rwkv7_mix(x, s_init, mu, w_r, w_k, w_v, w_o, w0, w_l1, w_l2, a0, a_l1, a_l2,
              g_l1, g_l2, k_k, k_a, r_k, ln_g, ln_b):
    b, n, d = x.shape
    x_prev, x_next = shift_neighbours(x)
    dx = 0.5 * (x_prev + x_next) - x
    xr, xw, xk, xv, xa, xg = [x + dx * mu[i] for i in range(6)]
    heads = lambda t: t.reshape(b, n, RWKV_H, RWKV_HS).astype(jnp.float32)
    r = heads(xr @ w_r)
    k = heads(xk @ w_k)
    v = heads(xv @ w_v)
    kk = k * k_k.reshape(RWKV_H, RWKV_HS).astype(jnp.float32)
    kk = kk * lax.rsqrt(jnp.sum(kk * kk, axis=-1, keepdims=True) + 1e-12)
    k_a_h = k_a.reshape(RWKV_H, RWKV_HS).astype(jnp.float32)
    r_k_f = r_k.astype(jnp.float32)
    g = jax.nn.sigmoid(xg @ g_l1) @ g_l2
    outs, bonuses, finals = [], [], []
    for dirn in range(2):
        logw = -jax.nn.softplus(-(w0[dirn] + jnp.tanh(xw @ w_l1[dirn]) @ w_l2[dirn])) - 0.5
        decay = heads(jnp.exp(-jnp.exp(logw.astype(jnp.float32))))
        a = heads(jax.nn.sigmoid(a0[dirn] + (xa @ a_l1[dirn]) @ a_l2[dirn]))
        k_eff = k * (1.0 + (a - 1.0) * k_a_h)
        s_fin, yd = wkv7_scan(s_init[:, dirn].astype(jnp.float32), r, decay, k_eff, v, kk, a, dirn == 1)
        outs.append(yd)
        bonuses.append(jnp.sum(r * k_eff * r_k_f, axis=-1, keepdims=True) * v)
        finals.append(s_fin)
    y = outs[0] + outs[1]
    mean = jnp.mean(y, axis=-1, keepdims=True)
    var = jnp.mean(jnp.square(y - mean), axis=-1, keepdims=True)
    y = ((y - mean) * lax.rsqrt(var + GN_EPS)).reshape(b, n, d) * ln_g + ln_b
    y = y + (bonuses[0] + bonuses[1]).reshape(b, n, d)
    out = (y.astype(x.dtype) * g) @ w_o
    return out, jnp.stack(finals, axis=1)

def rope_2d(x):
    n = x.shape[1]
    rows = n // GRID_W
    row = jnp.repeat(jnp.arange(rows), GRID_W)
    col = jnp.tile(jnp.arange(GRID_W), rows)
    pos = jnp.stack([row, col], axis=-1).astype(jnp.float32)
    quarter = D_ROPE // 4
    inv = ROPE_BASE ** (-jnp.arange(quarter, dtype=jnp.float32) / quarter)
    ang = pos[:, :, None] * inv
    cos = jnp.cos(ang)[:, None]
    sin = jnp.sin(ang)[:, None]
    xr = x.astype(jnp.float32).reshape(x.shape[:-1] + (2, 2, quarter))
    x1, x2 = xr[..., 0, :], xr[..., 1, :]
    out = jnp.stack([x1 * cos - x2 * sin, x1 * sin + x2 * cos], axis=-2)
    return out.reshape(x.shape).astype(x.dtype)

def mla_queries(x, w_dq, g_q, w_uq, positional):
    b, n, _ = x.shape
    q = (rmsnorm(x @ w_dq, g_q) @ w_uq).reshape(b, n, MLA_H, D_NOPE + D_ROPE)
    q_nope, q_rope = q[..., :D_NOPE], q[..., D_NOPE:]
    if positional:
        q_rope = rope_2d(q_rope)
    return q_nope, q_rope

def mla_compress(x, w_dkv, g_kv, positional):
    ckr = x @ w_dkv
    ckv = rmsnorm(ckr[..., :KV_RANK], g_kv)
    k_rope = ckr[..., KV_RANK:]
    if positional:
        k_rope = rope_2d(k_rope[:, :, None, :])[:, :, 0, :]
    return ckv, k_rope

def mla_attend(q_nope, q_rope, ckv, k_rope, w_uk, w_uv, w_o):
    b, nk, _ = ckv.shape
    k_nope = (ckv @ w_uk).reshape(b, nk, MLA_H, D_NOPE)
    v = (ckv @ w_uv).reshape(b, nk, MLA_H, D_V)
    s = (jnp.einsum('bqhd,bkhd->bhqk', q_nope, k_nope)
         + jnp.einsum('bqhr,bkr->bhqk', q_rope, k_rope)).astype(jnp.float32) * MLA_SCALE
    p = jax.nn.softmax(s, axis=-1).astype(v.dtype)
    o = jnp.einsum('bhqk,bkhd->bqhd', p, v)
    return o.reshape(b, -1, MLA_H * D_V) @ w_o

def setup_inputs(seed: int = 0) -> dict:
    key = jax.random.key(seed)
    ks = iter(jax.random.split(key, 64))
    D = D_MODEL

    def nrm(shape, scale):
        return jax.random.normal(next(ks), shape, jnp.float32) * scale

    def gain(shape):
        return 1.0 + nrm(shape, 0.1)

    return {
        "x_prompt": nrm((BATCH, SEQ, D), 1.0),
        "x_sample": nrm((DEC_BATCH, DEC_SEQ, D), 1.0),
        "state_rwkv": nrm((DEC_BATCH, N_RWKV_LAYERS, 2, RWKV_H, RWKV_HS, RWKV_HS), 0.3),
        "cache_mla_ckv": nrm((DEC_BATCH, N_MLA_LAYERS, PAST_LEN, KV_RANK), 1.0),
        "cache_mla_krope": nrm((DEC_BATCH, N_MLA_LAYERS, PAST_LEN, D_ROPE), 1.0),
        "c": nrm((DEC_BATCH, D), 1.0),
        "c_ctx": nrm((D,), 1.0),
        "mod_w": nrm((DEPTH, D, N_MOD * D), D ** -0.5),
        "mod_b": nrm((DEPTH, N_MOD * D), 0.1),
        "norm_g": gain((DEPTH, 4, D)),
        "mlp_w1": nrm((DEPTH, D, D_FF), D ** -0.5),
        "mlp_w2": nrm((DEPTH, D_FF, D), D_FF ** -0.5),
        "fft_w_out": nrm((N_FFT_LAYERS, D, D), D ** -0.5),
        "conv_w_in": nrm((N_CONV_LAYERS, D, 3 * D), D ** -0.5),
        "conv_w": nrm((N_CONV_LAYERS, 3, D), 3 ** -0.5),
        "conv_w_out": nrm((N_CONV_LAYERS, D, D), D ** -0.5),
        "rwkv_mu": jax.random.uniform(next(ks), (N_RWKV_LAYERS, 6, D), jnp.float32),
        "rwkv_w_r": nrm((N_RWKV_LAYERS, D, D), D ** -0.5),
        "rwkv_w_k": nrm((N_RWKV_LAYERS, D, D), D ** -0.5),
        "rwkv_w_v": nrm((N_RWKV_LAYERS, D, D), D ** -0.5),
        "rwkv_w_o": nrm((N_RWKV_LAYERS, D, D), D ** -0.5),
        "rwkv_w0": nrm((N_RWKV_LAYERS, 2, D), 0.5),
        "rwkv_w_l1": nrm((N_RWKV_LAYERS, 2, D, LORA_W), D ** -0.5),
        "rwkv_w_l2": nrm((N_RWKV_LAYERS, 2, LORA_W, D), 0.3 * LORA_W ** -0.5),
        "rwkv_a0": nrm((N_RWKV_LAYERS, 2, D), 0.5),
        "rwkv_a_l1": nrm((N_RWKV_LAYERS, 2, D, LORA_A), D ** -0.5),
        "rwkv_a_l2": nrm((N_RWKV_LAYERS, 2, LORA_A, D), 0.3 * LORA_A ** -0.5),
        "rwkv_g_l1": nrm((N_RWKV_LAYERS, D, LORA_G), D ** -0.5),
        "rwkv_g_l2": nrm((N_RWKV_LAYERS, LORA_G, D), LORA_G ** -0.5),
        "rwkv_k_k": gain((N_RWKV_LAYERS, D)),
        "rwkv_k_a": gain((N_RWKV_LAYERS, D)),
        "rwkv_r_k": nrm((N_RWKV_LAYERS, RWKV_H, RWKV_HS), 0.1),
        "rwkv_ln_g": gain((N_RWKV_LAYERS, D)),
        "rwkv_ln_b": nrm((N_RWKV_LAYERS, D), 0.02),
        "mla_w_dq": nrm((N_MLA_LAYERS, D, Q_RANK), D ** -0.5),
        "mla_g_q": gain((N_MLA_LAYERS, Q_RANK)),
        "mla_w_uq": nrm((N_MLA_LAYERS, Q_RANK, MLA_H * (D_NOPE + D_ROPE)), Q_RANK ** -0.5),
        "mla_w_dkv": nrm((N_MLA_LAYERS, D, KV_RANK + D_ROPE), D ** -0.5),
        "mla_g_kv": gain((N_MLA_LAYERS, KV_RANK)),
        "mla_w_uk": nrm((N_MLA_LAYERS, KV_RANK, MLA_H * D_NOPE), KV_RANK ** -0.5),
        "mla_w_uv": nrm((N_MLA_LAYERS, KV_RANK, MLA_H * D_V), KV_RANK ** -0.5),
        "mla_w_o": nrm((N_MLA_LAYERS, MLA_H * D_V, D), (MLA_H * D_V) ** -0.5),
    }

def reference(x_prompt, x_sample, state_rwkv, cache_mla_ckv, cache_mla_krope, c, c_ctx,
              mod_w, mod_b, norm_g, mlp_w1, mlp_w2,
              fft_w_out, conv_w_in, conv_w, conv_w_out,
              rwkv_mu, rwkv_w_r, rwkv_w_k, rwkv_w_v, rwkv_w_o, rwkv_w0, rwkv_w_l1, rwkv_w_l2,
              rwkv_a0, rwkv_a_l1, rwkv_a_l2, rwkv_g_l1, rwkv_g_l2, rwkv_k_k, rwkv_k_a, rwkv_r_k,
              rwkv_ln_g, rwkv_ln_b,
              mla_w_dq, mla_g_q, mla_w_uq, mla_w_dkv, mla_g_kv, mla_w_uk, mla_w_uv, mla_w_o):
    xp, xs = x_prompt, x_sample
    new_rwkv, new_ckv, new_krope = [], [], []
    for i in range(DEPTH):
        kind, j = i % N_MIXERS, i // N_MIXERS
        g4 = norm_g[i]
        m_ctx = modulation(c_ctx[None, :], mod_w[i], mod_b[i])
        m_lat = modulation(c, mod_w[i], mod_b[i])
        hp = rmsnorm(xp, g4[0]) * (1.0 + m_ctx[1]) + m_ctx[0]
        hs = rmsnorm(xs, g4[0]) * (1.0 + m_lat[1]) + m_lat[0]
        if kind == 0:
            op = fourier_mix(hp, fft_w_out[j])
            os_ = fourier_mix(hs, fft_w_out[j])
        elif kind == 1:
            op = short_conv_mix(hp, conv_w_in[j], conv_w[j], conv_w_out[j])
            os_ = short_conv_mix(hs, conv_w_in[j], conv_w[j], conv_w_out[j])
        elif kind == 2:
            rp = (rwkv_mu[j], rwkv_w_r[j], rwkv_w_k[j], rwkv_w_v[j], rwkv_w_o[j], rwkv_w0[j],
                  rwkv_w_l1[j], rwkv_w_l2[j], rwkv_a0[j], rwkv_a_l1[j], rwkv_a_l2[j],
                  rwkv_g_l1[j], rwkv_g_l2[j], rwkv_k_k[j], rwkv_k_a[j], rwkv_r_k[j],
                  rwkv_ln_g[j], rwkv_ln_b[j])
            s_zero = jnp.zeros((xp.shape[0], 2, RWKV_H, RWKV_HS, RWKV_HS), jnp.float32)
            op, s_ctx = rwkv7_mix(hp, s_zero, *rp)
            new_rwkv.append(s_ctx)
            os_, _ = rwkv7_mix(hs, state_rwkv[:, j], *rp)
        else:
            qn_p, qr_p = mla_queries(hp, mla_w_dq[j], mla_g_q[j], mla_w_uq[j], False)
            ckv_p, kr_p = mla_compress(hp, mla_w_dkv[j], mla_g_kv[j], False)
            new_ckv.append(ckv_p)
            new_krope.append(kr_p)
            op = mla_attend(qn_p, qr_p, ckv_p, kr_p, mla_w_uk[j], mla_w_uv[j], mla_w_o[j])
            qn_s, qr_s = mla_queries(hs, mla_w_dq[j], mla_g_q[j], mla_w_uq[j], True)
            ckv_s, kr_s = mla_compress(hs, mla_w_dkv[j], mla_g_kv[j], True)
            ckv_all = jnp.concatenate([cache_mla_ckv[:, j], ckv_s], axis=1)
            kr_all = jnp.concatenate([cache_mla_krope[:, j], kr_s], axis=1)
            os_ = mla_attend(qn_s, qr_s, ckv_all, kr_all, mla_w_uk[j], mla_w_uv[j], mla_w_o[j])
        xp = xp + m_ctx[2] * rmsnorm(op, g4[1])
        xs = xs + m_lat[2] * rmsnorm(os_, g4[1])
        hp = rmsnorm(xp, g4[2]) * (1.0 + m_ctx[4]) + m_ctx[3]
        hs = rmsnorm(xs, g4[2]) * (1.0 + m_lat[4]) + m_lat[3]
        fp = jnp.square(jax.nn.relu(hp @ mlp_w1[i])) @ mlp_w2[i]
        fs = jnp.square(jax.nn.relu(hs @ mlp_w1[i])) @ mlp_w2[i]
        xp = xp + m_ctx[5] * rmsnorm(fp, g4[3])
        xs = xs + m_lat[5] * rmsnorm(fs, g4[3])
    new_state_rwkv = jnp.stack(new_rwkv, axis=1)
    new_cache_mla_ckv = jnp.stack(new_ckv, axis=1)
    new_cache_mla_krope = jnp.stack(new_krope, axis=1)
    return (xp, xs, new_state_rwkv, new_cache_mla_ckv, new_cache_mla_krope)


_drawn_inputs = setup_inputs


def setup_inputs(seed=0):
    import zlib

    import numpy as np

    out = dict(_drawn_inputs(seed))
    spreads = {}
    factors = {'state_rwkv': 7.11, 'cache_mla_krope': 3.392, 'rwkv_ln_b': 8.0, 'mla_g_q': 7.387}
    for name, (base, spread) in spreads.items():
        noise = np.random.default_rng([zlib.crc32(name.encode()), seed]).standard_normal(out[name].shape)
        drawn = base * np.exp(spread * noise) if base else spread * noise
        out[name] = __import__('jax').numpy.asarray(drawn.astype(out[name].dtype))
    for name, factor in factors.items():
        out[name] = (out[name] * factor).astype(out[name].dtype)
    return out
```

```python
import math
from contextlib import ExitStack

import numpy as np

import concourse.bass as bass
import concourse.mybir as mybir

F32 = mybir.dt.float32
F32R = mybir.dt.float32r
U32 = mybir.dt.uint32
ALU = mybir.AluOpType
ACT = mybir.ActivationFunctionType
AX_X = mybir.AxisListType.X
AX_XY = mybir.AxisListType.XY

P = 128
D = 1024
KD = D // P
LAT, CTX = 512, 128
T = LAT + CTX
HT = T // 2
DEPTH = 4
NMOD = 6
D_FF = 4 * D
FB = 8
NFB = D_FF // P // FB
PIECES = ((0, HT, 0), (HT, LAT, 1), (LAT, T, 1))
SEG = ((0, LAT), (LAT, T))
MU = 3
MTILES = NMOD * KD
MSTEPS = MTILES // MU
EPS = 1e-6
PAST = 128
QR, KVR, DR, MH = 384, 256, 64, 8
TK = T + PAST
NH, HS = 16, 64
GRID_W, ROPE_BASE = 64, 10000.0
MLA_SCALE = (P + DR) ** -0.5
NQ, NKV = QR // P, KVR // P
MLA_IN = NQ + NKV + 1
KEYS = (((0, HT, 0, 0), (HT, LAT, 1, 0), (T, TK, 1, LAT - HT)), ((LAT, T, 0, 0),))
RWKV_IN = 3 + 3 * KD
ITEMS = ("act", "dve", "act", "act", "act", "dve", "dve", "dve", "act")
W = 128
NW = T // W
ITEMS_ACT, ITEMS_DVE = (NW * ITEMS.count(e) for e in ("act", "dve"))
DECAY = math.exp(-0.5)
GN_EPS = 64e-5

FFT_SLABS, CONV_SLABS, RWKV_SLABS, MLA_SLABS = 8, 32, 35, 24
MLP_SLABS = 2 * D_FF // P
SLABS = FFT_SLABS + CONV_SLABS + RWKV_SLABS + MLA_SLABS + DEPTH * MLP_SLABS


def halves(ap):
    return ap.rearrange("p (h n) -> p h n", h=2)


def build(nc, a, layers=(0, 1, 2, 3)):
    ctx = ExitStack()
    with ctx:
        cursor = [16512]

        def place(name, shape, dt=F32, at=None):
            size = 4 * int(np.prod(shape[1:]))
            if at is None:
                at = cursor[0]
                cursor[0] += (size + 31) // 32 * 32
            return nc.alloc_sbuf_tensor_at(name, shape, dt, offset=at)

        def after(at, *sizes):
            return at + sum((4 * s + 31) // 32 * 32 for s in sizes)

        x = place("x", [P, KD, T])
        acc = place("acc", [P, KD, T])
        hs_at = cursor[0]
        hs = place("hs", [P, KD, 2, T], F32R)
        fs_at = cursor[0]
        fs = place("fs", [P, FB, 2, T], F32R)
        ws_at = cursor[0]
        ws = place("ws", [P, 2, 2, KD * P], F32R)
        wr = place("wr", [P, 2, KD * P])
        mr_at = cursor[0]
        mr = place("mr", [P, MU, KD * P])
        sq_at = cursor[0]
        sq = place("sq", [P, 2, T])
        root = place("root", [P, T])
        rstd = place("rstd", [P, T])
        relu_at = cursor[0]
        relu = place("relu", [P, 2, T])
        ta = place("ta", [P, T])
        tb = place("tb", [P, T])
        ones = place("ones", [P, P])
        eps = place("eps", [P, 1])
        ident = place("ident", [P, P])
        sel = place("sel", [P, 2])
        cvec = place("cvec", [P, KD, 2])
        cgate = place("cgate", [P, KD, 2])
        cs = place("cs", [P, KD, 32])
        mpart = place("mpart", [P, MU * P])
        modt = place("modt", [P, MTILES, 2])
        modb = place("modb", [P, DEPTH, MTILES])
        ng = place("ng", [P, DEPTH, 4, KD])
        coef = place("coef", [P, NMOD, KD, 2])
        free_at = cursor[0]

        cw = place("cw", [P, 3, KD])
        gq = place("gq", [P, QR // P])
        gkv = place("gkv", [P, KVR // P])
        kro = place("kro", [P, CTX])
        mu = place("mu", [P, 6, KD])
        pv = place("pv", [P, 9, KD])
        pd = place("pd", [P, 5, KD])
        ewin = place("ewin", [P, KD, 2, 2, NW])
        eps_kk = place("eps_kk", [P, 1])
        eps_gn = place("eps_gn", [P, 1])
        free_at = cursor[0]
        zpad = place("zpad", [P, T + 4])
        conv = place("conv", [P, T + 2])

        cursor[0] = fs_at
        kn = place("kn", [P, MH, TK])
        qr = place("qr", [P, MH // 2, T])
        kr = place("kr", [P, TK])
        kvs = place("kvs", [P, KVR // P, 2, PAST], F32R)
        kvc = place("kvc", [P, KVR // P, PAST])
        assert cursor[0] <= fs_at + 4 * FB * 2 * T
        cursor[0] = mr_at
        pt_lat = place("pt_lat", [P, 5, LAT])
        pt_ctx = place("pt_ctx", [P, CTX])
        swap = place("swap", [P, P])
        ckvo = place("ckvo", [P, KVR // P, CTX])
        assert cursor[0] <= mr_at + 4 * MU * KD * P
        cos = place("cos", [P, LAT], at=relu_at)
        sin = place("sin", [P, LAT], at=relu_at + 4 * LAT)
        smax = place("smax", [P, 2, 2], at=relu_at + 8 * LAT)
        ssum = place("ssum", [P, 2, 2], at=relu_at + 8 * LAT + 32)
        cursor[0] = free_at
        vk = place("vk", [P, TK // P, MH * P])
        assert cursor[0] <= 229368, cursor[0]

        cursor[0] = mr_at
        tw = place("tw", [P, T])
        tav = place("tav", [P, T])
        tg = place("tg", [P, T])
        blk = place("blk", [P, P])
        l2 = place("l2", [P, 2, 3, P])
        assert cursor[0] <= mr_at + 4 * MU * KD * P
        cursor[0] = free_at
        dx = place("dx", [P, KD, T])
        cursor[0] = hs_at
        rkv = place("rkv", [P, 2, 3, T])
        kk = place("kk", [P, T])
        thw = place("thw", [P, 2, T])
        tha = place("tha", [P, 2, T])
        lw = place("lw", [P, T])
        cum = place("cum", [P, 2, T])
        ex = place("ex", [P, 2, 2, T])
        rate = place("rate", [P, 2, T])
        bvec = place("bvec", [P, T])
        tmix = place("tmix", [P, T])
        keff = place("keff", [P, 2, T])
        wmask = place("wmask", [P, T])
        ar0 = [place(f"ar0_{d}", [P, NW, 2, P]) for d in range(2)]
        bk0 = [place("bk0_0", [P, 2, T])]
        blocks = place("blocks", [P, 2 * NW, 32])
        assert cursor[0] <= ws_at
        cursor[0] = free_at
        e_in = place("e_in", [P, 2, T])
        e_ex = place("e_ex", [P, 2, T])
        e_neg = place("e_neg", [P, 2, T])
        bk0.append(place("bk0_1", [P, 2, T]))
        assert cursor[0] <= 229368
        cursor[0] = hs_at
        inv_a = place("inv_a", [P, 5, 32, 32])
        inv_x = place("inv_x", [P, 5, 32, 32])
        inv_t = place("inv_t", [P, 5 * 256])
        cursor[0] = fs_at
        ar = [place(f"ar_{d}", [P, NW, 2, P]) for d in range(2)]
        bk = [place("bk_0", [P, 2, T]), place("bk_1", [P, 2, T], at=hs_at + 4 * (KD - 1) * 2 * T)]
        xc = [place(f"xc_{d}", [P, 2 * NW, 32]) for d in range(2)]
        vd = place("vd", [P, T])
        dt_ = place("dt_", [P, 2 * NW, P])
        rhs = place("rhs", [P, NW, 2, 2, HS])
        tok = place("tok", [P, NW, 3, P])
        gt = place("gt", [P, NW, 2, P])
        wt = place("wt", [P, NW, P])
        assert cursor[0] <= ws_at + 4 * 2 * KD * P
        cursor[0] = free_at
        at_ = place("at_", [P, NW, 2, 4, P])
        yb = place("yb", [P, T])
        sb_ = place("sb_", [P, 2, P])
        assert cursor[0] <= 229368
        zz = place("zz", [P, NW, 2, 2, HS], at=relu_at)
        rp = place("rp", [P, NW, 2, 2, HS], at=sq_at)
        mask = place("mask", [P, 4 * P], U32, at=mr_at)
        s0 = place("s0", [P, 2, HS], at=mr_at + 4 * 4 * P)
        so = place("so", [P, 2, HS], at=mr_at + 4 * T)
        uu = place("uu", [P, P], at=mr_at + 4 * T + 8 * HS)

        dfeat = place("dfeat", [P, 2 * P], at=fs_at)
        dlat = place("dlat", [P, 2, LAT // P, LAT], at=after(fs_at, 2 * P))
        dctx = place("dctx", [P, 2, CTX], at=after(fs_at, 2 * P, 2 * LAT // P * LAT))
        yfeat = place("yfeat", [P, 2, NW, 2 * P], at=after(fs_at, 2 * P, 2 * LAT // P * LAT, 2 * CTX))

        if 2 in layers:
            rkv_d = nc.dram_tensor("rkv_d", [KD, 3, P, T], F32).ap()
            ar_d = nc.dram_tensor("ar_d", [2 * KD, P, 2 * T], F32).ap()
            bk_d = nc.dram_tensor("bk_d", [2 * KD, P, 2 * T], F32).ap()
            blk_d = nc.dram_tensor("blk_d", [P * 5 * 1024], F32).ap()
            inv_d = nc.dram_tensor("inv_d", [P * 5 * 1024], F32).ap()
            blk_v = blk_d.rearrange("(q n b c) -> q b n c", q=2 * KD, n=2 * NW, b=P, c=32)
            inv_v = inv_d.rearrange("(q n b c) -> q b n c", q=2 * KD, n=2 * NW, b=P, c=32)

        pu = ctx.enter_context(nc.psum_tensor("pu", [P, 2, 2, 512], F32))
        st = ctx.enter_context(nc.psum_tensor("st", [P, 2, 512], F32))
        pm = ctx.enter_context(nc.psum_tensor("pm", [P, 512], F32))
        pt = ctx.enter_context(nc.psum_tensor("pt", [P, 512], F32))

        def sem(name):
            return ctx.enter_context(nc.semaphore(name))

        consts_landed = sem("consts_landed")
        x_landed = sem("x_landed")
        w_landed = [sem("w_landed0"), sem("w_landed1")]
        m_landed = [sem(f"m_landed{j}") for j in range(MU)]
        hi_ready = sem("hi_ready")
        lo_ready = sem("lo_ready")
        tile_done = sem("tile_done")
        tile_read = sem("tile_read")
        mod_partial = sem("mod_partial")
        mod_copied = sem("mod_copied")
        mod_folded = sem("mod_folded")
        mod_added = sem("mod_added")
        gate_ready = sem("gate_ready")
        cs_ready = sem("cs_ready")
        sq_ready = sem("sq_ready")
        sq_summed = sem("sq_summed")
        root_ready = sem("root_ready")
        root_read = sem("root_read")
        x_ready = sem("x_ready")
        fhi_ready = sem("fhi_ready")
        h_ready = sem("h_ready")
        relu_ready = sem("relu_ready")
        eps_made = sem("eps_made")
        f_ready = sem("f_ready")
        yp_ready = sem("yp_ready")
        yf_ready = sem("yf_ready")
        x_stored = sem("x_stored")
        mla_landed = sem("mla_landed")
        rwkv_landed = sem("rwkv_landed")
        rkv_stored = [sem("rkv_stored0"), sem("rkv_stored1")]
        lora_ready = sem("lora_ready")
        b1_landed = [sem("b1_landed0"), sem("b1_landed1")]
        b1_z = sem("b1_z")
        b1_th = sem("b1_th")
        kksq_ready = sem("kksq_ready")
        kksq_summed = sem("kksq_summed")
        kk_root = sem("kk_root")
        e_ready = sem("e_ready")
        exps_ready = sem("exps_ready")
        prep_ready = sem("prep_ready")
        aab_done = sem("aab_done")
        blk_ready = sem("blk_ready")
        ab_stored = [sem("ab_stored0"), sem("ab_stored1")]
        blk_stored = sem("blk_stored")
        rk_ready = sem("rk_ready")
        bonus_summed = sem("bonus_summed")
        b1_done = sem("b1_done")
        b2_landed = sem("b2_landed")
        b2_done = sem("b2_done")
        x_inv_stored = sem("x_inv_stored")
        dt_ready = sem("dt_ready")
        b3_landed = [sem("b3_landed0"), sem("b3_landed1")]
        s0_landed = sem("s0_landed")
        l2_landed = sem("l2_landed")
        v_landed = sem("v_landed")
        vrev_ready = sem("vrev_ready")
        item_done = sem("item_done")
        item_seen = sem("item_seen")
        item_act = sem("item_act")
        item_dve = sem("item_dve")
        u_done = sem("u_done")
        u_ready = sem("u_ready")
        s_done = sem("s_done")
        s_ready = sem("s_ready")
        y_done = sem("y_done")
        y_read = sem("y_read")
        gn_sum = sem("gn_sum")
        gn_centred = sem("gn_centred")
        gn_sq = sem("gn_sq")
        gn_sum2 = sem("gn_sum2")
        gn_root = sem("gn_root")
        g_done = sem("g_done")
        b3_done = sem("b3_done")
        so_stored = sem("so_stored")
        masks_landed = sem("masks_landed")
        swap_done = sem("swap_done")
        swap_read = sem("swap_read")
        rope_done = sem("rope_done")
        cache_split = sem("cache_split")
        ckv_ready = sem("ckv_ready")
        kc_done = sem("kc_done")
        kc_read = sem("kc_read")
        scores_done = sem("scores_done")
        max_ready = sem("max_ready")
        exp_done = sem("exp_done")
        probs_ready = sem("probs_ready")
        turned = sem("turned")
        turned_copied = sem("turned_copied")
        pv_done = sem("pv_done")
        pv_read = sem("pv_read")

        block = ctx.enter_context(nc.Block())
        mixers = {0: FFT_SLABS, 1: CONV_SLABS, 2: RWKV_SLABS, 3: MLA_SLABS}
        n_consts = 3 * (0 in layers) + (1 in layers)
        n_slabs = sum(mixers[l] + MLP_SLABS for l in layers)

        @block.sync
        def _(sp):
            def load_w(s, i=0, step=0, f=0):
                if not (isinstance(i, int) and s < 2):
                    sp.wait_ge(lo_ready, s - 1 + step * i + 2 * FB * f)
                sp.dma_start(wr[:, s % 2, :], a["w_slabs"][s + step * i + 2 * FB * f]
                             ).then_inc(w_landed[s % 2], 16)

            def load_ws(s, n):
                if n > 1:
                    with sp.Fori(0, n // 2) as i:
                        for j in range(2):
                            load_w(s + j, i, 2)
                if n % 2:
                    load_w(s + n - 1)

            def load_m(n, i=0, f=0):
                if not (isinstance(i, int) and n == 0):
                    sp.wait_ge(mod_partial, n + i + FB // 2 * f)
                for j in range(MU):
                    sp.dma_start(mr[:, j, :], a["m_slabs"][MU * n + j + MU * i + MU * FB // 2 * f]
                                 ).then_inc(m_landed[j], 16)

            def load_const(name, t, landed):
                sp.dma_start(t[tuple(slice(None) for _ in t.shape)], a[name]).then_inc(landed, 16)

            for name, t in (("cvec", cvec), ("modb", modb), ("ng", ng), ("ones", ones), ("ident", ident),
                            ("sel", sel)):
                load_const(name, t, consts_landed)
            load_w(0)
            load_w(1)
            load_m(0)
            for k in range(KD):
                sp.dma_start(x[:, k, :], a["x"][k]).then_inc(x_landed, 16)
            if 1 in layers:
                load_const("cw", cw, x_landed)
            if 0 in layers:
                for name, t in (("dfeat", dfeat), ("dlat", dlat), ("dctx", dctx)):
                    load_const(name, t, x_landed)
            with sp.Fori(1, MSTEPS) as i:
                load_m(0, i)
            def rwkv_traffic(tiles):
                for stored in (blk_stored, so_stored):
                    sp.sem_inc(stored, 16)
                for stored in ab_stored:
                    sp.sem_inc(stored, 32)
                sp.wait_ge(tile_done, tiles)
                load_const("wmask", wmask, masks_landed)
                for j in range(2):
                    sp.wait_ge(rkv_stored[j], 16 * (3 * KD // 2))
                def load_tile(m, j):
                    sp.wait_ge(b1_done, m + 1)
                    sp.dma_start(rkv[:, j, :, :], rkv_d[m].rearrange("c p n -> p c n")).then_inc(b1_landed[j], 16)
                    sp.dma_start(l2[:, j, :, :], a["l2"][m]).then_inc(b1_landed[j], 16)

                def store_tile(m):
                    for d in range(2):
                        sp.wait_ge(prep_ready, 2 * m + d + 1)
                        sp.dma_start(ar_d[2 * m + d], ar0[d][:, :, :, :].rearrange("p w c n -> p (w c n)")
                                     ).then_inc(ab_stored[d], 16)
                        sp.dma_start(bk_d[2 * m + d], bk0[d][:, :, :].rearrange("p c n -> p (c n)")
                                     ).then_inc(ab_stored[d], 16)
                    for d in range(2):
                        sp.wait_ge(blk_ready, 2 * m + d + 2)
                        sp.dma_start(blk_v[2 * m + d], blocks[:, :, :]).then_inc(blk_stored, 16)

                load_tile(0, 0)
                load_tile(1, 1)
                with sp.Fori(0, KD // 2 - 1) as i:
                    for j in range(2):
                        store_tile(2 * i + j)
                        load_tile(2 * i + j + 2, j)
                for j in range(2):
                    store_tile(KD - 2 + j)
                sp.wait_ge(blk_stored, 16 * (2 * KD + 1))
                for stored in ab_stored:
                    sp.wait_ge(stored, 32 * (KD + 1))
                sp.wait_ge(b1_done, KD + 2)
                sp.dma_start(inv_a[:, :, :, :].rearrange("p q r c -> p (q r c)"),
                             blk_d.rearrange("(p n) -> p n", p=P)).then_inc(b2_landed, 16)
                sp.dma_start(mask[:, :], a["mask"]).then_inc(masks_landed, 16)
                sp.wait_ge(b2_done, 1)
                sp.dma_start(inv_d.rearrange("(p n) -> p n", p=P),
                             inv_x[:, :, :, :].rearrange("p q r c -> p (q r c)")).then_inc(x_inv_stored, 16)
                sp.wait_ge(x_inv_stored, 16)

                def load_operands(m, d):
                    sp.dma_start(ar[d][:, :, :, :].rearrange("p w c n -> p (w c n)"), ar_d[2 * m + d]
                                 ).then_inc(b3_landed[d], 16)
                    sp.dma_start(bk[d][:, :, :].rearrange("p c n -> p (c n)"), bk_d[2 * m + d]
                                 ).then_inc(b3_landed[d], 16)
                    sp.dma_start(xc[d][:, :, :], inv_v[2 * m + d]).then_inc(b3_landed[d], 16)

                sp.dma_start(vd[:, :], rkv_d[0, 2]).then_inc(v_landed, 16)
                load_operands(0, 0)
                sp.dma_start(s0[:, :, :], a["s0"][0]).then_inc(s0_landed, 16)
                load_operands(0, 1)
                sp.dma_start(l2[:, 0, :, :], a["l2"][0]).then_inc(l2_landed, 16)
                with sp.Fori(0, KD - 1) as m:
                    sp.wait_ge(vrev_ready, m + 1)
                    sp.dma_start(vd[:, :], rkv_d[m + 1, 2]).then_inc(v_landed, 16)
                    sp.wait_ge(y_done, NW * (2 * m + 1))
                    load_operands(m + 1, 0)
                    sp.wait_ge(s_ready, (NW + 1) * (2 * m + 1) + 2)
                    sp.dma_start(s0[:, :, :], a["s0"][m + 1]).then_inc(s0_landed, 16)
                    sp.wait_ge(y_done, NW * (2 * m + 2))
                    load_operands(m + 1, 1)
                    sp.wait_ge(s_ready, (NW + 1) * (2 * m + 2))
                    sp.dma_start(a["state"][m], so[:, :, :]).then_inc(so_stored, 16)
                    sp.wait_ge(g_done, m + 1)
                    sp.dma_start(l2[:, 0, :, :], a["l2"][m + 1]).then_inc(l2_landed, 16)
                sp.wait_ge(s_ready, (NW + 1) * 2 * KD)
                sp.dma_start(a["state"][KD - 1], so[:, :, :]).then_inc(so_stored, 16)
                sp.wait_ge(so_stored, 16 * (KD + 1))

            s, n = 2, MSTEPS
            tiles_before = 0
            for li, l in enumerate(layers):
                last = li == len(layers) - 1
                if l == 3:
                    sp.wait_ge(x_ready, 2 * KD * li)
                    for name, t in (("gq", gq), ("gkv", gkv), ("swap", swap), ("kvc", kvc), ("cos", cos), ("sin", sin)):
                        load_const(name, t, mla_landed)
                    for h in range(2):
                        sp.dma_start(kr[64 * h:64 * h + 64, T:TK], a["krc"]).then_inc(mla_landed, 16)
                if l == 2:
                    sp.wait_ge(x_ready, 2 * KD * li)
                    for name, t in (("mu", mu), ("pv", pv), ("blk", blk)):
                        load_const(name, t, rwkv_landed)
                    load_ws(s, RWKV_IN)
                    rwkv_traffic(tiles_before + RWKV_IN)
                    load_ws(s + RWKV_IN, RWKV_SLABS - RWKV_IN)
                else:
                    load_ws(s, mixers[l])
                s += mixers[l]
                tiles_before += {0: 2 * KD, 1: 4 * KD, 2: RWKV_SLABS, 3: 46}[l] + MLP_SLABS
                with sp.Fori(0, NFB - last) as f:
                    with sp.Fori(0, FB // 2) as i:
                        if not last:
                            load_m(n, i, f)
                        for j in range(2):
                            load_w(s + j, i, 2, f)
                    with sp.Fori(0, KD // 2) as i:
                        for j in range(2):
                            load_w(s + j + FB, i, 2, f)
                if last:
                    load_ws(s + 2 * FB * (NFB - 1), 2 * FB - 2)
                s, n = s + MLP_SLABS, n + MSTEPS
            for k in range(KD):
                sp.wait_ge(x_ready, 2 * KD * len(layers) - KD + k + 1)
                sp.dma_start(a["y"][k], x[:, k, :]).then_inc(x_stored, 16)
            if 3 in layers:
                sp.wait_ge(ckv_ready, 1)
                sp.dma_start(a["ckv"], ckvo[:, :, :]).then_inc(x_stored, 16)
                sp.dma_start(a["kr"], kro[0:DR, :]).then_inc(x_stored, 16)
                sp.wait_ge(x_stored, 16 * 2)
            sp.wait_ge(x_stored, 16 * (KD + 2 * (3 in layers)))

        @block.gpsimd
        def _(pool):
            def low_part(s, i=0, step=0):
                pool.wait_ge(hi_ready, s + 1 + step * i)
                pool.tensor_tensor(ws[:, s % 2, 1, :], wr[:, s % 2, :], ws[:, s % 2, 0, :].bitcast(F32),
                                   ALU.subtract).then_inc(lo_ready, 1)
            even = n_slabs // 2 * 2
            with pool.Fori(0, even // 2) as i:
                for j in range(2):
                    low_part(j, i, 2)
            if n_slabs % 2:
                low_part(n_slabs - 1)

        @block.tensor
        def _(pe):
            tile = [0]
            slab = [0]
            norm = [0]
            squares = [0]
            step = [0]
            h_tiles = [0]
            f_tiles = [0]

            def split_matmuls(out, w_hi, w_lo, r_hi, r_lo, first, last):
                for i, (wt, rt) in enumerate(((w_hi, r_hi), (w_hi, r_lo), (w_lo, r_hi))):
                    for h in range(2):
                        mm = pe.matmul(out[:, h, 0:HT], wt, rt[:, h * HT:(h + 1) * HT],
                                       start=(first and i == 0), stop=(last and i == 2))
                return mm

            def unit(src, s, t, i=0, ready=None, ready_at=0):
                pe.wait_ge(lo_ready, s + 1 + i)
                if not (isinstance(i, int) and t < 2):
                    pe.wait_ge(tile_read, t - 1 + i)
                for k in range(KD):
                    if ready is not None:
                        pe.wait_ge(ready, ready_at + k + 1)
                    mm = split_matmuls(pu[:, t % 2], ws[:, s % 2, 0, k * P:(k + 1) * P],
                                       ws[:, s % 2, 1, k * P:(k + 1) * P], src[:, k, 0, :], src[:, k, 1, :],
                                       k == 0, k == KD - 1)
                mm.then_inc(tile_done, 1)

            def units(src, n, ready, ready_at):
                s, t = slab[0], tile[0]
                with pe.Fori(0, n, 2) as i:
                    unit(src, s, t, i, ready, ready_at)
                    unit(src, s + 1, t + 1, i)
                slab[0] += n
                tile[0] += n

            def norm_sums(n_tiles=KD):
                if norm[0]:
                    pe.wait_ge(root_ready, norm[0])
                for k in range(n_tiles):
                    m = squares[0]
                    pe.wait_ge(sq_ready, m + 1)
                    for h in range(2):
                        mm = pe.matmul(st[:, h, 0:HT], ones[:, :], sq[:, m % 2, h * HT:(h + 1) * HT],
                                       start=(k == 0), stop=(k == n_tiles - 1))
                    mm.then_inc(sq_summed, 1)
                    squares[0] += 1
                norm[0] += 1

            def mod_partials(n, i=0):
                if not (isinstance(i, int) and n == 0):
                    pe.wait_ge(mod_copied, n + i)
                for j in range(MU):
                    pe.wait_ge(m_landed[j], 16 * (n + 1) + 16 * i)
                    for k in range(KD):
                        g = k % 4
                        mm = pe.matmul(pm[32 * g:32 * g + 32, j * P:(j + 1) * P], cs[:, k, :],
                                       mr[:, j, k * P:(k + 1) * P], start=(k < 4), stop=(k >= 4),
                                       tile_position=(0, 32 * g), skip_group_check=True)
                mm.then_inc(mod_partial, 1)

            def mod_fold(n, i=0):
                pe.wait_ge(mod_copied, n + 1 + i)
                if not (isinstance(i, int) and n == 0):
                    pe.wait_ge(mod_added, n + i)
                for j in range(MU):
                    mm = pe.matmul(pt[:, 2 * j:2 * j + 2], mpart[:, j * P:(j + 1) * P], sel[:, :],
                                   start=True, stop=True)
                mm.then_inc(mod_folded, 1)

            def fourier():
                NL = LAT // P

                def over_features(g):
                    pe.wait_ge(h_ready, h_tiles[0] + g + 1)
                    if g:
                        pe.wait_ge(yf_ready, g)
                    for n in range(NW):
                        o = (st[:, n // 2, (n % 2) * 256:(n % 2) * 256 + 256] if n < 4 else pm[:, 0:256])
                        mm = pe.matmul(o, acc[:, g, n * P:(n + 1) * P], dfeat[:, :], start=True, stop=True,
                                       skip_group_check=True)
                    mm.then_inc(yp_ready, 1)

                def over_tokens(g):
                    pe.wait_ge(yf_ready, g + 1)
                    t = tile[0]
                    if t >= 2:
                        pe.wait_ge(tile_read, t - 1)
                    for n in range(NL):
                        for c in range(2):
                            pe.matmul(pu[:, t % 2, 0, :], yfeat[:, g % 2, n, c * P:(c + 1) * P], dlat[:, c, n, :],
                                      start=(n + c == 0), stop=(n + c == NL))
                    for c in range(2):
                        mm = pe.matmul(pu[:, t % 2, 1, 0:CTX], yfeat[:, g % 2, NL, c * P:(c + 1) * P], dctx[:, c, :],
                                       start=(c == 0), stop=(c == 1))
                    mm.then_inc(tile_done, 1)
                    tile[0] += 1

                over_features(0)
                for g in range(KD):
                    if g < KD - 1:
                        over_features(g + 1)
                    over_tokens(g)
                h_tiles[0] += KD
                units(hs, KD, tile_read, tile[0] - KD)

            def short_conv():
                units(hs, 3 * KD, h_ready, h_tiles[0])
                h_tiles[0] += KD
                units(fs, KD, f_ready, f_tiles[0])
                f_tiles[0] += KD

            def rwkv():
                h0 = h_tiles[0] + KD
                for i, n in enumerate((1, 1, 1, KD, KD, KD)):
                    src = (hs, fs)[i % 2]
                    if n == 1:
                        unit(src, slab[0], tile[0], 0, h_ready, h0 + i * KD)
                        slab[0] += 1
                        tile[0] += 1
                    else:
                        units(src, n, h_ready, h0 + i * KD)
                h_tiles[0] += 7 * KD
                pe.wait_ge(tile_read, tile[0])
                pe.wait_ge(lora_ready, 1)
                pe.wait_ge(rwkv_landed, 16 * 3)
                pe.wait_ge(root_ready, norm[0])

                def wide(out, w, rows, src):
                    for h in range(2):
                        mm = pe.matmul(out[:, h, 0:HT], w[rows], src[rows][:, h * HT:(h + 1) * HT], start=True, stop=True)
                    return mm

                pe.sem_inc(aab_done, 2)

                def prepare(m, j, i):
                    pe.wait_ge(b1_landed[j], 32 * (i + 1))
                    pe.wait_ge(b1_done, m + 2)
                    for d in range(2):
                        rows = slice(64 * d, 64 * d + 64)
                        if d:
                            pe.wait_ge(b1_th, 2 * m + 1)
                        wide(pu[:, 0], l2[:, j, 0, :], rows, tw)
                        wide(pu[:, 1], l2[:, j, 1, :], rows, tav).then_inc(b1_z, 1)
                        if d == 0:
                            pe.wait_ge(kksq_ready, m + 1)
                            pe.wait_ge(blk_ready, 2 * m + 1)
                            wide(st, blk[:, :], slice(0, P), tb).then_inc(kksq_summed, 1)
                    pe.wait_ge(b1_th, 2 * m + 2)
                    pe.wait_ge(rk_ready, m + 1)
                    wide(pu[:, 0], blk[:, :], slice(0, P), ta).then_inc(bonus_summed, 1)
                    for d in range(2):
                        pe.wait_ge(blk_ready, 2 * m + d + 1)
                        pe.wait_ge(prep_ready, 2 * m + d + 1)
                        for n in range(2 * NW):
                            w, h = n // 2, n % 2
                            r = slice(64 * h, 64 * h + 64)
                            out = (pm, pt)[h][:, 0:P] if w == 4 else st[:, h, w * P:(w + 1) * P]
                            mm = pe.matmul(out, ar0[d][r, w, 0, :], bk0[d][r, 0, w * P:(w + 1) * P], start=True, stop=True,
                                           skip_group_check=True)
                        mm.then_inc(aab_done, 1)

                with pe.Fori(0, KD // 2) as i:
                    for j in range(2):
                        prepare(2 * i + j, j, i)

                pe.wait_ge(b1_done, KD + 2)
                pe.wait_ge(masks_landed, 32)

                def norm_start(m):
                    pe.wait_ge(y_read, 2 * NW * m)
                    wide(st, blk[:, :], slice(0, P), yb).then_inc(gn_sum, 1)
                    pe.wait_ge(l2_landed, 16 * m)
                    for h in range(2):
                        mm = pe.matmul((pm, pt)[h][:, 0:HT], l2[:, 0, 2, :], tg[:, h * HT:(h + 1) * HT], start=True, stop=True)
                    mm.then_inc(g_done, 1)

                def norm_end(m):
                    pe.wait_ge(gn_sq, m)
                    wide(st, blk[:, :], slice(0, P), root).then_inc(gn_sum2, 1)

                windows(0, 0, None, None)
                windows(0, 1, None, None)
                with pe.Fori(1, KD) as m:
                    windows(m, 0, norm_start, norm_end)
                    windows(m, 1, None, None)
                norm_start(KD)
                norm_end(KD)
                units(hs, KD, b3_done, 1)

            def windows(m, d, norm_start, norm_end):
                q = 2 * m + d

                def wait_items(n_act, n_dve):
                    pe.wait_ge(item_act, ITEMS_ACT * q + n_act + 1)
                    pe.wait_ge(item_dve, ITEMS_DVE * q + n_dve + 1)

                def bank(n):
                    return pu[:, n % 4 // 2, n % 2, :]

                def count(n, kind):
                    return sum(ITEMS[j // NW] == kind for j in range(max(n, 0)))

                if norm_start:
                    norm_start(m)
                pe.wait_ge(b3_landed[d], 48 * (m + 1))
                if d:
                    pe.wait_ge(vrev_ready, m + 1)
                else:
                    pe.wait_ge(v_landed, 16 * (m + 1))
                v = tb if d else vd
                n = 0
                for w in range(NW):
                    wait_items(count(n - 3, "act"), 0)
                    c = slice(w * P, (w + 1) * P)
                    for j, src in enumerate((ar[d][:, w, 0, :], bk[d][:, 0, c], bk[d][:, 1, c], v[:, c])):
                        mm = pe.transpose(bank(n)[:, j * P:(j + 1) * P], src, ident[:, :])
                    mm.then_inc(item_done, 1)
                    n += 1
                for w in range(NW):
                    wait_items(NW, max(w - 1, 0))
                    c = slice(w * P, (w + 1) * P)
                    for h in range(2):
                        r = slice(64 * h, 64 * h + 64)
                        out = pu[:, w % 2, h, :]
                        pe.matmul(out[:, 0:P], ar[d][r, w, 0, :], bk[d][r, 0, c], start=True, stop=True, skip_group_check=True)
                        pe.matmul(out[:, P:3 * P], bk[d][r, 1, c], ar[d][r, w, :, :].rearrange("p c n -> p (c n)"), start=True,
                                  stop=True, skip_group_check=True)
                        mm = pe.matmul(out[:, 3 * P:4 * P], bk[d][r, 0, c], ar[d][r, w, 1, :], start=True, stop=True,
                                       skip_group_check=True)
                    mm.then_inc(item_done, 1)
                    n += 1
                    if norm_end and w == 2:
                        norm_end(m)
                pe.wait_ge(dt_ready, q + 1)

                def pairs(n, w_of, r_of, by_head=True):
                    for w in range(NW):
                        wait_items(count(n - 3, "act"), max(NW if n < 14 else 0, count(n - 3, "dve")))
                        for h in range(2):
                            out = bank(n)[:, h * P:(h + 1) * P]
                            if not by_head:
                                out = bank(n)[:, 0:2 * P].rearrange("p (c h n) -> p c h n", c=2, h=2)[:, :, h, :]
                            mm = pe.matmul(out, w_of(w, h), r_of(w, h), start=True, stop=True,
                                           skip_group_check=True)
                        mm.then_inc(item_done, 1)
                        n += 1
                    return n

                n = pairs(n, lambda w, h: at_[:, w, h, 0, :], lambda w, h: dt_[:, 2 * w + h, :])
                n = pairs(n, lambda w, h: at_[:, w, h, 1, :], lambda w, h: tok[:, w, 2, :])
                n = pairs(n, lambda w, h: dt_[:, 2 * w + h, :], lambda w, h: rhs[:, w, :, h, :], False)
                for i in range(3):
                    n = pairs(n, lambda w, h: gt[:, w, h, :], lambda w, h: (zz if i else rp)[:, w, :, h, :], False)
                for w in range(NW):
                    wait_items(count(n - 3, "act"), count(n - 3, "dve"))
                    pe.transpose(bank(n)[:, 0:P], zz[:, w, 0, :, :].rearrange("p h n -> p (h n)"), ident[:, :]).then_inc(item_done, 1)
                    n += 1
                if d == 0:
                    pe.wait_ge(b3_done, m + 1)
                for w in range(NW):
                    wq = NW * q + w
                    pe.wait_ge(item_act, ITEMS_ACT * q + count(41 + w, "act") + 1)
                    pe.wait_ge(s_ready, (NW + 1) * q + w + 1)
                    pe.wait_ge(u_ready, wq + 1)
                    pe.matmul(pm[:, 0:P], wt[:, w, :], sb_[:, w % 2, :], start=True, stop=True).then_inc(u_done, 1)
                    pe.wait_ge(u_ready, wq + 2)
                    pe.matmul(pt[:, 0:P], tok[:, w, 0, :], uu[:, :], start=True, stop=False)
                    pe.matmul(pt[:, 0:P], tok[:, w, 1, :], tok[:, w, 2, :], start=False, stop=True).then_inc(s_done, 1)
                    if w >= 2:
                        pe.wait_ge(y_read, wq - 1)
                    y = st[:, w % 2, 0:P]
                    pe.matmul(y, sb_[:, w % 2, :], ar[d][:, w, 1, :], start=True, stop=False, skip_group_check=True)
                    for h in range(2):
                        r = slice(64 * h, 64 * h + 64)
                        pe.matmul(y[r], uu[:, r], at_[:, w, h, 3, :], start=False, stop=False, skip_group_check=True)
                        mm = pe.matmul(y[r], tok[:, w, 2, r], at_[:, w, h, 2, :], start=False, stop=True,
                                       skip_group_check=True)
                    mm.then_inc(y_done, 1)

            def latent_attention():
                units(hs, MLA_IN, h_ready, h_tiles[0])
                h_tiles[0] += KD
                norm_sums(NQ)
                norm_sums(NKV)
                pe.wait_ge(mla_landed, 16 * 8)

                def swapped(n, src, at):
                    pe.wait_ge(tile_read, at)
                    if n:
                        pe.wait_ge(swap_read, n)
                    pe.matmul(pt[:, 0:LAT], swap[:, :], src, start=True, stop=True).then_inc(swap_done, 1)

                def product(j, nk, w_at, src, s):
                    t = tile[0]
                    pe.wait_ge(tile_read, t - 1)
                    for k in range(nk):
                        c = w_at + k * P
                        mm = split_matmuls(pu[:, t % 2], ws[:, s % 2, 0, c:c + P], ws[:, s % 2, 1, c:c + P],
                                           src(k)[:, 0, :], src(k)[:, 1, :], k == 0, k == nk - 1)
                    mm.then_inc(tile_done, 1)
                    tile[0] += 1

                t_kr = tile[0]
                swapped(0, kr[:, 0:LAT], t_kr)
                pe.wait_ge(h_ready, h_tiles[0] + NQ)
                t_q = tile[0]
                for _ in range(6):
                    pe.wait_ge(lo_ready, slab[0] + 1)
                    for j in range(2):
                        product(j, NQ, j * QR, lambda k: hs[:, k], slab[0])
                    slab[0] += 1
                for j in range(MH // 2):
                    swapped(1 + j, qr[:, j, 0:LAT], t_q + MH + j + 1)
                pe.wait_ge(h_ready, h_tiles[0] + NQ + NKV)
                pe.wait_ge(cache_split, 1)
                h_tiles[0] += NQ + NKV
                for b in range(2):
                    s = slab[0]
                    pe.wait_ge(lo_ready, s + 1)
                    if b:
                        pe.wait_ge(kc_read, b)
                    for j in range(4):
                        for k in range(NKV):
                            c = j * KVR + k * P
                            for i, (wp, rp) in enumerate(((0, 0), (0, 1), (1, 0))):
                                mm = pe.matmul(pm[:, j * P:(j + 1) * P], ws[:, s % 2, wp, c:c + P], kvs[:, k, rp, :],
                                               start=(k + i == 0), stop=(k == NKV - 1 and i == 2))
                    mm.then_inc(kc_done, 1)
                    for j in range(4):
                        product(j, NKV, j * KVR, lambda k: hs[:, NQ + k], s)
                    slab[0] += 1
                for b in range(2):
                    s = slab[0]
                    pe.wait_ge(lo_ready, s + 1)
                    for kt in range(TK // P):
                        t = tile[0]
                        pe.wait_ge(tile_read, t - 1)
                        for k in range(NKV):
                            for i, (xp, wp) in enumerate(((0, 0), (0, 1), (1, 0))):
                                keys = kvs[:, k, xp, :] if kt == NW else hs[:, NQ + k, xp, kt * P:(kt + 1) * P]
                                mm = pe.matmul(pu[:, t % 2, 0, :], keys, ws[:, s % 2, wp, k * 512:(k + 1) * 512],
                                               start=(k + i == 0), stop=(k == NKV - 1 and i == 2))
                        mm.then_inc(tile_done, 1)
                        tile[0] += 1
                    slab[0] += 1
                pe.wait_ge(tile_read, tile[0])
                pe.wait_ge(rope_done, 5)
                pe.wait_ge(kc_read, 2)

                def scores(n):
                    h, q = n // 5, n % 5
                    if n >= 2:
                        pe.wait_ge(exp_done, n - 1)
                    r = 64 * (h % 2)
                    for c, (p, e, b, o) in enumerate(KEYS[q == 4]):
                        out = pu[:, n % 2, b, o:o + e - p]
                        pe.matmul(out, acc[:, h, q * P:(q + 1) * P], kn[:, h, p:e], start=(o == 0), stop=False,
                                  skip_group_check=True)
                    for c, (p, e, b, o) in enumerate(KEYS[q == 4]):
                        out = pu[:, n % 2, b, o:o + e - p]
                        mm = pe.matmul(out, qr[r:r + 64, h // 2, q * P:(q + 1) * P], kr[r:r + 64, p:e],
                                       start=False, stop=True, skip_group_check=True)
                    mm.then_inc(scores_done, 1)

                def turn(n):
                    pe.wait_ge(probs_ready, n + 1)
                    if n:
                        pe.wait_ge(turned_copied, n)
                    p = (ta, tb)[n % 2]
                    for kt in range(1 if n % 5 == 4 else 5):
                        mm = pe.transpose(st[:, kt // 4, (kt % 4) * P:(kt % 4 + 1) * P], p[:, kt * P:(kt + 1) * P],
                                          ident[:, :])
                    mm.then_inc(turned, 1)

                def values(h):
                    pe.wait_ge(turned_copied, 5 * h + 5)
                    if h:
                        pe.wait_ge(pv_read, h)
                    for i, kt in enumerate((0, 1, 2, 3, 5)):
                        pe.matmul(pm[:, 0:LAT], vk[:, kt, h * P:(h + 1) * P], pt_lat[:, i, :],
                                  start=(i == 0), stop=(i == 4))
                    pe.matmul(pt[:, 0:CTX], vk[:, 4, h * P:(h + 1) * P], pt_ctx[:, :], start=True, stop=True
                              ).then_inc(pv_done, 1)

                n_items = 5 * MH
                scores(0)
                for n in range(n_items):
                    if n + 1 < n_items:
                        scores(n + 1)
                    turn(n)
                    if n % 5 == 0 and n:
                        values(n // 5 - 1)
                values(MH - 1)
                units(hs, KD, pv_read, 0)

            def mlp(last):
                s, t, n = slab[0], tile[0], step[0]
                with pe.Fori(0, NFB) as f:
                    with pe.Fori(0, FB // 2) as i:
                        at, m_at = 2 * FB * f + 2 * i, FB // 2 * f + i
                        if not last:
                            mod_partials(n, m_at)
                        unit(hs, s, t, at, h_ready, h_tiles[0])
                        if not last:
                            mod_fold(n, m_at)
                        unit(hs, s + 1, t + 1, at)
                    with pe.Fori(0, KD // 2) as i:
                        at = 2 * FB * f + FB + 2 * i
                        unit(fs, s, t, at, f_ready, f_tiles[0] + FB * f)
                        unit(fs, s + 1, t + 1, at)
                slab[0] += MLP_SLABS
                tile[0] += MLP_SLABS
                h_tiles[0] += KD
                f_tiles[0] += NFB * FB
                if not last:
                    step[0] += MSTEPS

            pe.wait_ge(consts_landed, 16 * 6)
            pe.wait_ge(cs_ready, 1)
            mod_partials(0)
            mod_fold(0)
            with pe.Fori(1, MSTEPS) as i:
                mod_partials(0, i)
                mod_fold(0, i)
            step[0] = MSTEPS
            pe.wait_ge(x_landed, 16 * (KD + n_consts))
            norm_sums()
            for li, l in enumerate(layers):
                (fourier, short_conv, rwkv, latent_attention)[l]()
                norm_sums()
                norm_sums()
                mlp(li == len(layers) - 1)
                norm_sums()
                if li < len(layers) - 1:
                    norm_sums()

        @block.scalar
        def _(act):
            tile = [0]
            slab = [0]
            norm = [0]
            squares = [0]
            x_tiles = [0]
            f_tiles = [0]

            def high_part(s, used, i=0):
                act.wait_ge(w_landed[s % 2], 16 * (s // 2 + 1) + 8 * i)
                if used is not None:
                    act.wait_ge(tile_done, used + i)
                act.activation(ws[:, s % 2, 0, :], wr[:, s % 2, :], ACT.Copy).then_inc(hi_ready, 1)

            def keep_ahead(n):
                s, t = slab[0], tile[0]
                left = min(n, n_slabs - 1 - s)
                if s == 0:
                    high_part(1, None)
                    high_part(2, t + 1)
                else:
                    high_part(s + 1, t)
                    high_part(s + 2, t + 1)
                if left > 3:
                    with act.Fori(2, left // 2 * 2, 2) as i:
                        high_part(s + 1, t, i)
                        high_part(s + 2, t + 1, i)
                if left % 2:
                    high_part(s + left, t + left - 1)
                slab[0] += n
                tile[0] += n

            def norm_squares(src, ready, at, n=KD, first=0):
                for k in range(n):
                    if ready is not None:
                        act.wait_ge(ready, at + k + 1)
                    m = squares[0]
                    if m >= 2:
                        act.wait_ge(sq_summed, m - 1)
                    act.activation(sq[:, m % 2, :], src[:, first + k, :], ACT.Square).then_inc(sq_ready, 1)
                    squares[0] += 1
                act.wait_ge(sq_summed, squares[0])
                if norm[0]:
                    act.wait_ge(root_read, norm[0])
                act.activation(halves(root[:, :]), st[:, :, 0:HT], ACT.Sqrt, bias=eps[:, :],
                               scale=1.0 / (n * P)).then_inc(root_ready, 1)
                norm[0] += 1

            def fourier():
                for g in range(KD):
                    act.wait_ge(yp_ready, g + 1)
                    if g >= 2:
                        act.wait_ge(tile_done, tile[0] + g - 1)
                    for b in range(2):
                        act.activation(yfeat[:, g % 2, 2 * b:2 * b + 2, :],
                                       st[:, b, :].rearrange("p (n c) -> p n c", n=2), ACT.Copy)
                    act.activation(yfeat[:, g % 2, 4, :], pm[:, 0:2 * P], ACT.Copy).then_inc(yf_ready, 1)
                tile[0] += KD
                keep_ahead(KD)

            def rwkv():
                act.sem_inc(item_act, 1)
                s, t = slab[0], tile[0]
                for j, (dst, f, sc) in enumerate(((tw, ACT.Tanh, 1.0), (tav, ACT.Copy, 1.0), (tg, ACT.Tanh, 0.5))):
                    high_part(s + 1 + j, t + j)
                    act.wait_ge(tile_done, t + j + 1)
                    act.activation(halves(dst[:, :]), pu[:, (t + j) % 2, :, 0:HT], f, scale=sc).then_inc(tile_read, 1)
                s, t = s + 3, t + 3

                def project(j, i, c, m):
                    high_part(s + 1 + j, t + j, 2 * i)
                    act.wait_ge(tile_done, t + j + 1 + 2 * i)
                    if not (isinstance(i, int) and j < 2):
                        act.wait_ge(rkv_stored[j % 2], 16 * (j // 2) + 16 * i)
                    act.activation(halves(relu[:, j % 2, :]), pu[:, (t + j) % 2, :, 0:HT], ACT.Copy).then_inc(tile_read, 1)
                    act.wait_ge(tile_read, t + j + 1 + 2 * i)
                    act.dma_start(rkv_d[m, c], relu[:, j % 2, :]).then_inc(rkv_stored[j % 2], 16)

                for c in range(3):
                    for j in range(2):
                        project(KD * c + j, 0, c, j)
                    with act.Fori(1, KD // 2) as i:
                        for j in range(2):
                            project(KD * c + j, i, c, 2 * i + j)
                slab[0], tile[0] = s + 3 * KD, t + 3 * KD

                act.sem_inc(blk_ready, 1)
                with act.Fori(0, KD) as m:
                    col = bass.ds(m, 1)
                    for d in range(2):
                        act.wait_ge(b1_z, 2 * m + d + 1)
                        act.wait_ge(e_ready, 2 * m + d + 1)
                        act.activation(halves(thw[:, d, :]), pu[:, 0, :, 0:HT], ACT.Tanh, scale=0.5, bias=pd[:, d, col])
                        act.activation(halves(tha[:, d, :]), pu[:, 1, :, 0:HT], ACT.Tanh, scale=0.5, bias=pd[:, 2 + d, col]
                                       ).then_inc(b1_th, 1)
                    act.wait_ge(kksq_summed, m + 1)
                    act.activation(halves(root[:, :]), st[:, :, 0:HT], ACT.Sqrt, bias=eps_kk[:, :]).then_inc(kk_root, 1)
                    for d in range(2):
                        act.wait_ge(e_ready, 2 * m + d + 3)
                        act.activation(e_in[:, d, :], ex[:, d, 0, :], ACT.Exp)
                        act.activation(e_ex[:, d, :], ex[:, d, 1, :], ACT.Exp)
                        act.activation(ewin[:, col, d, 0, :].rearrange("p m w -> p (m w)"), cum[:, d, 63:T:W], ACT.Exp)
                        act.activation(ewin[:, col, d, 1, :].rearrange("p m w -> p (m w)"), ex[:, d, 0, W - 1:T:W], ACT.Exp)
                        act.activation(e_neg[:, d, :], ex[:, d, 0, :], ACT.Exp, scale=-1.0).then_inc(exps_ready, 1)
                    for d in range(2):
                        act.wait_ge(aab_done, 2 * m + d + 3)
                        act.wait_ge(blk_stored, 16 * (2 * m + d + 1))
                        for b in range(4):
                            r = slice(32 * b, 32 * b + 32)
                            dst = blocks[r, :, :].rearrange("p (w h) c -> p h w c", h=2)
                            act.activation(dst[:, :, 0:4, :], st[r, :, :].rearrange("p h (w c) -> p h w c", w=4)[:, :, :, r],
                                           ACT.Copy)
                            act.activation(dst[:, 0, 4, :], pm[r, r], ACT.Copy)
                            op = act.activation(dst[:, 1, 4, :], pt[r, r], ACT.Copy)
                        op.then_inc(blk_ready, 1)

                def head_norm(m):
                    act.wait_ge(gn_centred, m)
                    act.activation(root[:, :], ta[:, :], ACT.Square).then_inc(gn_sq, 1)
                    act.wait_ge(gn_sum2, m)
                    act.activation(halves(root[:, :]), st[:, :, 0:HT], ACT.Sqrt, bias=eps_gn[:, :], scale=1.0 / HS
                                   ).then_inc(gn_root, 1)

                def scan_tile(m, first):
                    for d in range(2):
                        q = 2 * m + d
                        for kind in (0, 2, 3, 4, 8):
                            if kind == 2 and d == 0 and not first:
                                head_norm(m)
                            for w in range(NW):
                                n = kind * NW + w
                                act.wait_ge(item_done, len(ITEMS) * NW * q + n + 1)
                                b = pu[:, n % 4 // 2, n % 2, :]
                                if kind == 0:
                                    act.activation(rhs[:, w, 0, :, :].rearrange("p h n -> p (h n)"), b[:, 0:P], ACT.Copy)
                                    op = act.activation(tok[:, w, :, :].rearrange("p c n -> p (c n)"), b[:, P:4 * P], ACT.Copy)
                                elif kind == 2:
                                    op = act.activation(gt[:, w, :, :].rearrange("p h n -> p (h n)"), b[:, 0:2 * P], ACT.Copy)
                                elif kind == 3:
                                    op = act.activation(rhs[:, w, 1, :, :],
                                                        b[:, 0:384].rearrange("p (h n) -> p h n", h=2)[:, :, 0:HS], ACT.Copy)
                                elif kind == 4:
                                    op = act.activation(rp[:, w, :, :, :].rearrange("p c h n -> p (c h n)"), b[:, 0:2 * P], ACT.Copy)
                                else:
                                    op = act.activation(wt[:, w, :], b[:, 0:P], ACT.Copy)
                                op.then_inc(item_act, 1)

                scan_tile(0, True)
                with act.Fori(1, KD) as m:
                    scan_tile(m, False)
                head_norm(KD)
                keep_ahead(KD)

            def latent_attention():
                s0, t0 = slab[0], tile[0]
                used = [t0 + 1 + j for j in range(MLA_IN)]
                used += [t0 + MLA_IN + 2 * (j + 1) for j in range(6)]
                used += [used[-1] + 4, used[-1] + 8, used[-1] + 14, used[-1] + 20]
                for j in range(1, MLA_IN + 1):
                    high_part(s0 + j, used[j - 2] if j >= 2 else t0)
                norm_squares(acc, tile_read, t0, NQ)
                norm_squares(acc, tile_read, t0 + NQ, NKV, NQ)
                for j in range(MLA_IN + 1, 17):
                    high_part(s0 + j, used[j - 2])
                slab[0], tile[0] = s0 + 16, used[15]

                def exponent(n):
                    act.wait_ge(max_ready, n + 1)
                    if n >= 2:
                        act.wait_ge(turned, n - 1)
                    p = (ta, tb)[n % 2]
                    if n % 5 == 4:
                        src, dst = pu[:, n % 2, 0, 0:CTX], p[:, 0:CTX]
                    else:
                        src, dst = pu[:, n % 2, :, 0:HT], halves(p[:, :])
                    act.activation(dst, src, ACT.Exp, bias=smax[:, n % 2, 1:2], scale=MLA_SCALE,
                                   accum_out=ssum[:, n % 2, 0:1]).then_inc(exp_done, 1)

                def copy_turned(n):
                    act.wait_ge(turned, n + 1)
                    q, h = n % 5, n // 5
                    if q == 4:
                        act.activation(pt_ctx[:, :], st[:, 0, 0:CTX], ACT.Copy).then_inc(turned_copied, 1)
                        return
                    if q == 0 and h:
                        act.wait_ge(pv_done, h)
                    act.activation(pt_lat[:, 0:4, q * P:(q + 1) * P], st[:, 0, :].rearrange("p (k n) -> p k n", k=4),
                                   ACT.Copy)
                    act.activation(pt_lat[:, 4, q * P:(q + 1) * P], st[:, 1, 0:P], ACT.Copy).then_inc(turned_copied, 1)

                n_items = 5 * MH
                exponent(0)
                for n in range(n_items):
                    if n + 1 < n_items:
                        exponent(n + 1)
                    copy_turned(n)
                keep_ahead(KD)

            def mlp(last):
                s, t, f0 = slab[0], tile[0], f_tiles[0]

                def hidden(t, i, f, j):
                    act.wait_ge(tile_done, t + 1 + 2 * i + 2 * FB * f)
                    act.wait_ge(tile_read, t - 1 + 2 * i + 2 * FB * f)
                    act.activation(halves(relu[:, j, :]), pu[:, t % 2, :, 0:HT], ACT.Relu).then_inc(relu_ready, 1)
                    act.drain()
                    act.activation(fs[:, 2 * i + j, 0, :], relu[:, j, :], ACT.Square).then_inc(fhi_ready, 1)

                def block_of(f, units_ahead):
                    with act.Fori(0, FB // 2) as i:
                        for j in range(2):
                            high_part(s + 1 + j, t + j, 2 * i + 2 * FB * f)
                            hidden(t + j, i, f, j)
                    with act.Fori(0, units_ahead // 2) as i:
                        for j in range(2):
                            high_part(s + FB + 1 + j, t + FB + j, 2 * i + 2 * FB * f)
                    if units_ahead % 2:
                        high_part(s + FB + units_ahead, t + FB + units_ahead - 1, 2 * FB * f)

                with act.Fori(0, NFB - last) as f:
                    block_of(f, KD)
                if last:
                    block_of(NFB - 1, KD - 1)
                slab[0] += MLP_SLABS
                tile[0] += MLP_SLABS
                f_tiles[0] += NFB * FB

            act.wait_ge(consts_landed, 16 * 6)
            act.activation(cgate[:, :, :], cvec[:, :, :], ACT.Tanh, scale=0.5).then_inc(gate_ready, 1)
            high_part(0, None)
            act.wait_ge(x_landed, 16 * (KD + n_consts))
            act.wait_ge(eps_made, 1)
            norm_squares(x, None, 0)
            for li, l in enumerate(layers):
                last = li == len(layers) - 1
                if l == 0:
                    fourier()
                if l == 3:
                    latent_attention()
                if l == 2:
                    rwkv()
                if l == 1:
                    keep_ahead(CONV_SLABS)
                    f_tiles[0] += KD
                norm_squares(acc, tile_read, tile[0] - KD)
                norm_squares(x, x_ready, x_tiles[0])
                x_tiles[0] += KD
                mlp(last)
                norm_squares(acc, tile_read, tile[0] - KD)
                x_tiles[0] += KD
                if not last:
                    norm_squares(x, x_ready, x_tiles[0] - KD)

        @block.vector
        def _(dve):
            tile = [0]
            norm = [0]
            step = [0]
            hidden = [0]

            def take_root():
                dve.wait_ge(root_ready, norm[0] + 1)
                dve.reciprocal(rstd[:, :], root[:, :]).then_inc(root_read, 1)
                dve.drain()
                norm[0] += 1

            def add_normed(c):
                take_root()
                for k in range(KD):
                    t = (ta, tb)[k % 2]
                    dve.tensor_tensor(t[:, :], acc[:, k, :], rstd[:, :], ALU.mult)
                    dve.drain()
                    for g, (p, q) in enumerate(SEG):
                        op = dve.scalar_tensor_tensor(x[:, k, p:q], t[:, p:q], coef[:, c, k, g:g + 1], x[:, k, p:q],
                                                      ALU.mult, ALU.add)
                    op.then_inc(x_ready, 1)

            def modulate(ca, cb, plain):
                take_root()
                if tile[0]:
                    dve.wait_ge(tile_done, tile[0])
                for k in range(KD):
                    dve.tensor_tensor(ta[:, :], x[:, k, :], rstd[:, :], ALU.mult)
                    dve.drain()
                    h = acc[:, k, :] if plain else tb[:, :]
                    for g, (p, q) in enumerate(SEG):
                        op = dve.tensor_scalar(h[:, p:q], ta[:, p:q], coef[:, ca, k, g:g + 1], coef[:, cb, k, g:g + 1],
                                               ALU.mult, ALU.add)
                    if plain:
                        op.then_inc(h_ready, 1)
                    dve.drain()
                    if plain:
                        continue
                    dve.tensor_copy(hs[:, k, 0, :], h)
                    dve.drain()
                    dve.tensor_tensor(hs[:, k, 1, :], h, hs[:, k, 0, :].bitcast(F32), ALU.subtract
                                      ).then_inc(h_ready, 1)

            def copy_out(n):
                for m in range(n):
                    t = tile[0]
                    dve.wait_ge(tile_done, t + 1)
                    dve.tensor_copy(halves(acc[:, m, :]), pu[:, t % 2, :, 0:HT]).then_inc(tile_read, 1)
                    tile[0] += 1

            def mod_copy(n, i=0):
                dve.wait_ge(mod_partial, n + 1 + i)
                if not (isinstance(i, int) and n == 0):
                    dve.wait_ge(mod_folded, n + i)
                dve.tensor_copy(mpart[:, :], pm[:, 0:MU * P]).then_inc(mod_copied, 1)

            def mod_add(layer, n, at, i=0):
                dve.wait_ge(mod_folded, n + 1 + i)
                dve.tensor_tensor(modt[:, bass.ds(at, MU), :], pt[:, 0:2 * MU].rearrange("p (j g) -> p j g", g=2),
                                  modb[:, layer, bass.ds(at, MU)].unsqueeze(2).to_broadcast([P, MU, 2]),
                                  ALU.add).then_inc(mod_added, 1)

            def coefficients(l):
                dve.drain()
                for c, part, gain in ((0, 1, 0), (2, 2, 1), (3, 4, 2), (5, 5, 3)):
                    dve.scalar_tensor_tensor(coef[:, c, :, :], modt[:, part * KD:(part + 1) * KD, :],
                                             0.0 if c in (2, 5) else 1.0,
                                             ng[:, l, gain, :].unsqueeze(2).to_broadcast([P, KD, 2]),
                                             ALU.add, ALU.mult)
                for c, part in ((1, 0), (4, 3)):
                    dve.tensor_copy(coef[:, c, :, :], modt[:, part * KD:(part + 1) * KD, :])
                dve.drain()

            def split_out(dst, m):
                t = tile[0]
                dve.wait_ge(tile_done, t + 1)
                for part, (p, q) in enumerate(SEG):
                    dve.tensor_copy(dst[:, m, 0, p:q], pu[:, t % 2, part, 0:q - p])
                dve.drain()
                for part, (p, q) in enumerate(SEG):
                    op = dve.tensor_tensor(dst[:, m, 1, p:q], pu[:, t % 2, part, 0:q - p],
                                           dst[:, m, 0, p:q].bitcast(F32), ALU.subtract)
                op.then_inc(tile_read, 1)
                tile[0] += 1

            def fourier():
                for g in range(KD):
                    split_out(hs, g)
                copy_out(KD)

            def padded(buf, p, q, shift=0):
                at = p + shift + (0 if p < LAT else 2)
                return buf[:, at:at + q - p]

            def short_conv():
                dve.memset(zpad[:, :], 0.0)
                dve.drain()
                t0 = tile[0]
                with dve.Fori(0, KD // 2) as i:
                    for half in range(2):
                        m = 2 * i + half
                        psum = []
                        for j in range(3):
                            psum.append(pu[:, (t0 + 3 * half + j) % 2])
                        at = t0 + 3 * half + 6 * i
                        dve.wait_ge(tile_done, at + 1)
                        dve.tensor_copy(halves(ta[:, :]), psum[0][:, :, 0:HT]).then_inc(tile_read, 1)
                        dve.drain()
                        dve.wait_ge(tile_done, at + 2)
                        for p, q, h in PIECES:
                            op = dve.tensor_tensor(padded(zpad, p, q, 1), ta[:, p:q],
                                                   psum[1][:, h, p - h * HT:q - h * HT], ALU.mult)
                        op.then_inc(tile_read, 1)
                        dve.drain()
                        dve.tensor_scalar(conv[:, :], zpad[:, 1:T + 3], cw[:, 1, bass.ds(m, 1)], None, ALU.mult)
                        dve.drain()
                        for tap, off in ((0, 0), (2, 2)):
                            dve.scalar_tensor_tensor(conv[:, :], zpad[:, off:off + T + 2], cw[:, tap, bass.ds(m, 1)],
                                                     conv[:, :], ALU.mult, ALU.add)
                            dve.drain()
                        dve.wait_ge(tile_done, at + 3)
                        for p, q, h in PIECES:
                            op = dve.tensor_tensor(tb[:, p:q], padded(conv, p, q),
                                                   psum[2][:, h, p - h * HT:q - h * HT], ALU.mult)
                        op.then_inc(tile_read, 1)
                        dve.drain()
                        dve.tensor_copy(fs[:, m, 0, :], tb[:, :])
                        dve.drain()
                        dve.tensor_tensor(fs[:, m, 1, :], tb[:, :], fs[:, m, 0, :].bitcast(F32), ALU.subtract
                                          ).then_inc(f_ready, 1)
                tile[0] += 3 * KD
                copy_out(KD)

            def rwkv():
                for done in (b3_done, item_dve, u_ready):
                    dve.sem_inc(done, 1)
                for done in (b1_done, e_ready):
                    dve.sem_inc(done, 2)
                dve.memset(eps_kk[:, :], 1e-12)
                dve.memset(eps_gn[:, :], GN_EPS)
                dve.wait_ge(rwkv_landed, 16 * 3)
                dve.tensor_scalar(pd[:, 0:4, :], pv[:, 0:4, :], 0.5, None, ALU.mult)
                dve.tensor_scalar(pd[:, 4, :], pv[:, 5, :], -1.0, 1.0, ALU.mult, ALU.add)
                for p, q in SEG:
                    dve.tensor_tensor(dx[:, :, p + 1:q - 1], acc[:, :, p:q - 2], acc[:, :, p + 2:q], ALU.add)
                    dve.tensor_copy(dx[:, :, p:p + 1], acc[:, :, p + 1:p + 2])
                    dve.tensor_copy(dx[:, :, q - 1:q], acc[:, :, q - 2:q - 1])
                dve.drain()
                dve.scalar_tensor_tensor(dx[:, :, :].rearrange("p k n -> p (k n)"), dx[:, :, :].rearrange("p k n -> p (k n)"),
                                         0.5, acc[:, :, :].rearrange("p k n -> p (k n)"), ALU.mult, ALU.subtract)
                dve.drain()
                t_in = tile[0]
                for i, (which, before) in enumerate(((1, 0), (4, 0), (5, 1), (0, 2), (2, 3), (3, 3 + KD))):
                    dst = (hs, fs)[i % 2]
                    if before:
                        dve.wait_ge(tile_done, t_in + before)
                    for k in range(KD):
                        dve.scalar_tensor_tensor(ta[:, :], dx[:, k, :], mu[:, which, k:k + 1], acc[:, k, :], ALU.mult, ALU.add)
                        dve.drain()
                        dve.tensor_copy(dst[:, k, 0, :], ta[:, :])
                        dve.drain()
                        dve.tensor_tensor(dst[:, k, 1, :], ta[:, :], dst[:, k, 0, :].bitcast(F32), ALU.subtract
                                          ).then_inc(h_ready, 1)
                        dve.drain()
                    if i == 3:
                        dve.wait_ge(tile_read, t_in + 3)
                        dve.tensor_scalar(tg[:, :], tg[:, :], 0.5, 0.5, ALU.mult, ALU.add).then_inc(lora_ready, 1)
                tile[0] += RWKV_IN
                dve.wait_ge(tile_done, tile[0])
                dve.wait_ge(masks_landed, 16)

                def by_window(ap):
                    return ap.rearrange("p (w n) -> p w n", w=NW)

                def prepare(m, j, i):
                    col = bass.ds(m, 1)

                    def way(ap, d):
                        return ap[:, ::-1] if d else ap

                    dve.wait_ge(b1_landed[j], 32 * (i + 1))
                    r, k, v = (rkv[:, j, c, :] for c in range(3))
                    dve.tensor_scalar(kk[:, :], k, pv[:, 4, col], None, ALU.mult)
                    dve.drain()
                    dve.tensor_tensor(tb[:, :], kk[:, :], kk[:, :], ALU.mult).then_inc(kksq_ready, 1)
                    for d in range(2):
                        q = 2 * m + d
                        dve.wait_ge(b1_th, q + 1)
                        dve.tensor_scalar(lw[:, :], way(thw[:, d, :], d), -DECAY / 2, -DECAY / 2, ALU.mult, ALU.add)
                        dve.tensor_scalar(rate[:, d, :], tha[:, d, :], 0.5, 0.5, ALU.mult, ALU.add)
                        dve.drain()
                        dve.tensor_tensor_scan(cum[:, d, :], wmask[:, :], lw[:, :], 0.0, ALU.mult, ALU.add)
                        dve.tensor_scalar(tmix[:, :], rate[:, d, :], pv[:, 5, col], pd[:, 4, col], ALU.mult, ALU.add)
                        dve.drain()
                        dve.tensor_tensor(by_window(ex[:, d, 0, :]), by_window(cum[:, d, :]),
                                          by_window(cum[:, d, :])[:, :, 63:64].to_broadcast([P, NW, W]), ALU.subtract)
                        dve.tensor_tensor(keff[:, d, :], k, tmix[:, :], ALU.mult)
                        dve.drain()
                        dve.tensor_tensor(ex[:, d, 1, :], ex[:, d, 0, :], lw[:, :], ALU.subtract).then_inc(e_ready, 1)
                        dve.drain()
                    dve.tensor_tensor(tmix[:, :], keff[:, 0, :], keff[:, 1, :], ALU.add)
                    dve.drain()
                    dve.scalar_tensor_tensor(ta[:, :], r, pv[:, 6, col], tmix[:, :], ALU.mult, ALU.mult).then_inc(rk_ready, 1)
                    dve.wait_ge(kk_root, m + 1)
                    dve.reciprocal(rstd[:, :], root[:, :])
                    dve.drain()
                    dve.tensor_tensor(kk[:, :], kk[:, :], rstd[:, :], ALU.mult)
                    dve.drain()
                    for d in range(2):
                        q = 2 * m + d
                        dve.tensor_tensor(bvec[:, :], kk[:, :], rate[:, d, :], ALU.mult)
                        dve.wait_ge(exps_ready, q + 1)
                        dve.wait_ge(ab_stored[d], 32 * m + 32)
                        dve.wait_ge(aab_done, q + 1)
                        dve.scalar_tensor_tensor(ar0[d][:, :, 0, :], by_window(way(kk[:, :], d)), -1.0,
                                                 by_window(e_ex[:, d, :]), ALU.mult, ALU.mult)
                        dve.tensor_tensor(ar0[d][:, :, 1, :], by_window(way(r, d)), by_window(e_in[:, d, :]), ALU.mult)
                        dve.drain()
                        dve.tensor_tensor(bk0[d][:, 1, :], way(keff[:, d, :], d), e_neg[:, d, :], ALU.mult)
                        dve.tensor_tensor(bk0[d][:, 0, :], way(bvec[:, :], d), e_neg[:, d, :], ALU.mult).then_inc(prep_ready, 1)
                        dve.drain()
                        if d == 0:
                            dve.wait_ge(bonus_summed, m + 1)
                            dve.tensor_tensor(halves(acc[:, col, :].rearrange("p m n -> p (m n)")), pu[:, 0, :, 0:HT],
                                              halves(v), ALU.mult)
                    dve.sem_inc(b1_done, 1)

                with dve.Fori(0, KD // 2) as i:
                    for j in range(2):
                        prepare(2 * i + j, j, i)

                dve.wait_ge(b2_landed, 16)
                dve.memset(inv_x[:, :, :, :], 0.0)
                dve.drain()
                dve.memset(inv_x[:, :, :, :].rearrange("p q r c -> p q (r c)")[:, :, 0:1024:33], 1.0)
                dve.drain()
                for j in range(31):
                    n = 31 - j
                    t = inv_t[:, 0:5 * n * (j + 1)].rearrange("p (q r c) -> p q r c", q=5, r=n)
                    shape = [P, 5, n, j + 1]
                    dve.tensor_tensor(t, inv_a[:, :, j + 1:32, j:j + 1].to_broadcast(shape),
                                      inv_x[:, :, j:j + 1, 0:j + 1].to_broadcast(shape), ALU.mult)
                    dve.drain()
                    rows = inv_x[:, :, j + 1:32, 0:j + 1]
                    dve.tensor_tensor(rows, rows, t, ALU.add)
                    dve.drain()
                dve.sem_inc(b2_done, 1)
                dve.wait_ge(masks_landed, 32)
                dve.wait_ge(x_inv_stored, 16)
                dve.memset(at_[:, :, :, :, :], 0.0)
                dve.memset(dt_[:, :, :], 0.0)
                dve.memset(sb_[:, :, :], 0.0)
                dve.drain()

                def centre(m):
                    dve.wait_ge(gn_sum, m)
                    dve.scalar_tensor_tensor(halves(ta[:, :]), st[:, :, 0:HT], -1.0 / HS, halves(yb[:, :]), ALU.mult, ALU.add
                                             ).then_inc(gn_centred, 1)

                def finish(m):
                    col = bass.ds(m - 1, 1)
                    dve.wait_ge(gn_root, m)
                    dve.reciprocal(rstd[:, :], root[:, :])
                    dve.drain()
                    dve.tensor_tensor(tb[:, :], ta[:, :], rstd[:, :], ALU.mult)
                    dve.drain()
                    dve.tensor_scalar(ta[:, :], tb[:, :], pv[:, 7, col], pv[:, 8, col], ALU.mult, ALU.add)
                    dve.drain()
                    dve.tensor_tensor(tb[:, :], ta[:, :], acc[:, col, :].rearrange("p m n -> p (m n)"), ALU.add)
                    dve.drain()
                    dve.wait_ge(g_done, m)
                    for h in range(2):
                        c = slice(h * HT, (h + 1) * HT)
                        dve.tensor_tensor(ta[:, c], (pm, pt)[h][:, 0:HT], tb[:, c], ALU.mult)
                    dve.drain()
                    dve.tensor_copy(hs[:, col, 0, :].rearrange("p m n -> p (m n)"), ta[:, :])
                    dve.drain()
                    dve.tensor_tensor(hs[:, col, 1, :].rearrange("p m n -> p (m n)"), ta[:, :],
                                      hs[:, col, 0, :].rearrange("p m n -> p (m n)").bitcast(F32), ALU.subtract
                                      ).then_inc(b3_done, 1)
                    dve.drain()

                def scan_tile(m, first):
                    col = bass.ds(m, 1)
                    for d in range(2):
                        q = 2 * m + d
                        dve.wait_ge(b3_landed[d], 48 * (m + 1))
                        for b in range(4):
                            rr = slice(32 * b, 32 * b + 32)
                            op = dve.transpose(dt_[rr, :, rr], xc[d][rr, :, :])
                        op.then_inc(dt_ready, 1)
                        if d == 0 and not first:
                            centre(m)
                        base = len(ITEMS) * NW * q
                        for w in range(NW):
                            dve.wait_ge(item_done, base + NW + w + 1)
                            dve.sem_inc(item_seen, 1)
                            dve.copy_predicated(at_[:, w, :, :, :].rearrange("p h c n -> p h (c n)"),
                                                mask[:, :].unsqueeze(1).to_broadcast([P, 2, 4 * P]),
                                                pu[:, w % 2, :, :]).then_inc(item_dve, 1)
                        lat0 = 1 if d else 0
                        ctx_w = 0 if d else NW - 1

                        def start(w, slot):
                            dve.memset(sb_[:, slot, :], 0.0)
                            dve.drain()
                            if w == lat0:
                                for h in range(2):
                                    r = slice(64 * h, 64 * h + 64)
                                    dve.tensor_scalar(sb_[r, slot, r], s0[r, d, :], ewin[r, col, d, 0, w:w + 1].rearrange(
                                        "p m w -> p (m w)"), None, ALU.mult)
                                dve.drain()
                            dve.sem_inc(s_ready, 1)

                        if d == 0:
                            dve.wait_ge(s0_landed, 16 * (m + 1))
                        start(0, 0)
                        if d == 0:
                            if not first:
                                finish(m)
                            dve.wait_ge(v_landed, 16 * (m + 1))
                            dve.tensor_copy(tb[:, :], vd[:, ::-1]).then_inc(vrev_ready, 1)
                        for i in range(3):
                            for w in range(NW):
                                n = 5 * NW + i * NW + w
                                dve.wait_ge(item_done, base + n + 1)
                                dve.tensor_tensor(zz[:, w, :, :, :].rearrange("p c h n -> p (c h n)"),
                                                  pu[:, n % 4 // 2, n % 2, 0:2 * P],
                                                  rp[:, w, :, :, :].rearrange("p c h n -> p (c h n)"), ALU.add).then_inc(item_dve, 1)
                        for w in range(NW):
                            wq = NW * q + w
                            dve.wait_ge(u_done, wq + 1)
                            dve.tensor_tensor(uu[:, :].rearrange("p (h n) -> p h n", h=2),
                                              pm[:, 0:P].rearrange("p (h n) -> p h n", h=2), zz[:, w, 1, :, :], ALU.add
                                              ).then_inc(u_ready, 1)
                            dve.wait_ge(s_done, wq + 1)
                            ec = ewin[:, col, d, 1, w:w + 1].rearrange("p m w -> p (m w)")
                            if w == ctx_w:
                                if d == 0:
                                    dve.wait_ge(so_stored, 16 * m + 16)
                                for h in range(2):
                                    r = slice(64 * h, 64 * h + 64)
                                    op = dve.tensor_scalar(so[r, d, :], pt[r, r], ec[r], None, ALU.mult)
                            if w == NW - 1:
                                if w == ctx_w:
                                    op.then_inc(s_ready, 1)
                                else:
                                    dve.sem_inc(s_ready, 1)
                            elif w == ctx_w:
                                start(w + 1, (w + 1) % 2)
                            elif w + 1 == ctx_w:
                                start(w + 1, (w + 1) % 2)
                            else:
                                nxt = (w + 1) % 2
                                em = ewin[:, col, d, 0, w + 1:w + 2].rearrange("p m w -> p (m w)")
                                for h in range(2):
                                    r = slice(64 * h, 64 * h + 64)
                                    dve.tensor_tensor(sb_[r, nxt, r], pt[r, r], sb_[r, w % 2, r], ALU.add)
                                dve.drain()
                                dve.tensor_scalar(sb_[:, nxt, :], sb_[:, nxt, :], ec, em, ALU.mult, ALU.mult).then_inc(s_ready, 1)
                            dve.wait_ge(y_done, wq + 1)
                            y = st[:, w % 2, 0:P]
                            if d:
                                out = yb[:, T - (w + 1) * W:T - w * W]
                                dve.tensor_tensor(out[:, ::-1], y, out[:, ::-1], ALU.add).then_inc(y_read, 1)
                            else:
                                dve.tensor_copy(yb[:, w * W:(w + 1) * W], y).then_inc(y_read, 1)

                scan_tile(0, True)
                with dve.Fori(1, KD) as m:
                    scan_tile(m, False)
                centre(KD)
                finish(KD)
                copy_out(KD)

            def latent_attention():
                t0 = tile[0]

                def take_tile(dst, whole=True):
                    t = tile[0]
                    dve.wait_ge(tile_done, t + 1)
                    src = pu[:, t % 2, :, 0:HT] if whole else pu[:, t % 2, 0, :]
                    dve.tensor_copy(halves(dst) if whole else dst, src).then_inc(tile_read, 1)
                    tile[0] += 1

                def gained(k, n, gain):
                    dve.tensor_tensor(ta[:, :], acc[:, k, :], rstd[:, :], ALU.mult)
                    dve.drain()
                    dve.tensor_scalar(tb[:, :], ta[:, :], gain[:, n:n + 1], None, ALU.mult)
                    dve.drain()
                    dve.tensor_copy(hs[:, k, 0, :], tb[:, :])
                    if k >= NQ:
                        dve.tensor_copy(ckvo[:, n, :], tb[:, LAT:T])
                    dve.drain()
                    dve.tensor_tensor(hs[:, k, 1, :], tb[:, :], hs[:, k, 0, :].bitcast(F32), ALU.subtract
                                      ).then_inc(h_ready, 1)

                def rotate(n, buf):
                    dve.tensor_tensor(ta[:, 0:LAT], buf, cos[:, :], ALU.mult)
                    dve.wait_ge(swap_done, n + 1)
                    dve.tensor_tensor(tb[:, 0:LAT], pt[:, 0:LAT], sin[:, :], ALU.mult).then_inc(swap_read, 1)
                    dve.drain()
                    dve.tensor_tensor(buf, ta[:, 0:LAT], tb[:, 0:LAT], ALU.add).then_inc(rope_done, 1)
                    dve.drain()

                for k in range(NQ + NKV):
                    take_tile(acc[:, k, :])
                take_tile(kr[:, 0:T])
                dve.drain()
                dve.tensor_copy(kro[:, :], kr[:, LAT:T])
                dve.wait_ge(mla_landed, 16 * 8)
                take_root()
                for k in range(NQ):
                    gained(k, k, gq)
                take_root()
                for k in range(NKV):
                    gained(NQ + k, k, gkv)
                dve.drain()
                dve.tensor_copy(kvs[:, :, 0, :], kvc[:, :, :]).then_inc(ckv_ready, 1)
                dve.drain()
                dve.tensor_tensor(kvs[:, :, 1, :], kvc[:, :, :], kvs[:, :, 0, :].bitcast(F32), ALU.subtract
                                  ).then_inc(cache_split, 1)
                rotate(0, kr[:, 0:LAT])
                for h in range(MH):
                    take_tile(acc[:, h, :])
                for j in range(MH // 2):
                    take_tile(qr[:, j, :])
                dve.drain()
                for j in range(MH // 2):
                    rotate(1 + j, qr[:, j, 0:LAT])
                for b in range(2):
                    dve.wait_ge(kc_done, b + 1)
                    dve.tensor_copy(kn[:, 4 * b:4 * b + 4, T:TK], pm[:, :].rearrange("p (h n) -> p h n", h=4)
                                    ).then_inc(kc_read, 1)
                    for j in range(4):
                        take_tile(kn[:, 4 * b + j, 0:T])
                for b in range(2):
                    for kt in range(TK // P):
                        take_tile(vk[:, kt, b * 512:(b + 1) * 512], False)

                def maximum(n):
                    dve.wait_ge(scores_done, n + 1)
                    src = pu[:, n % 2, 0, 0:CTX] if n % 5 == 4 else pu[:, n % 2, :, 0:HT]
                    dve.tensor_reduce(smax[:, n % 2, 0:1], src, AX_X if n % 5 == 4 else AX_XY, ALU.max)
                    dve.drain()
                    dve.tensor_scalar(smax[:, n % 2, 1:2], smax[:, n % 2, 0:1], -MLA_SCALE, None, ALU.mult
                                      ).then_inc(max_ready, 1)

                def normalise(n):
                    dve.wait_ge(exp_done, n + 1)
                    dve.reciprocal(ssum[:, n % 2, 1:2], ssum[:, n % 2, 0:1])
                    dve.drain()
                    p = (ta, tb)[n % 2]
                    p = p[:, 0:CTX] if n % 5 == 4 else p[:, :]
                    dve.tensor_scalar(p, p, ssum[:, n % 2, 1:2], None, ALU.mult).then_inc(probs_ready, 1)

                def take_values(h):
                    dve.wait_ge(pv_done, h + 1)
                    src = (pm[:, 0:LAT], pt[:, 0:CTX])
                    for g, (p, q) in enumerate(SEG):
                        dve.tensor_copy(hs[:, h, 0, p:q], src[g])
                    dve.drain()
                    for g, (p, q) in enumerate(SEG):
                        op = dve.tensor_tensor(hs[:, h, 1, p:q], src[g], hs[:, h, 0, p:q].bitcast(F32), ALU.subtract)
                    op.then_inc(pv_read, 1)

                n_items = 5 * MH
                maximum(0)
                for n in range(n_items):
                    if n + 1 < n_items:
                        maximum(n + 1)
                    normalise(n)
                    if n % 5 == 1 and n > 5:
                        take_values(n // 5 - 1)
                take_values(MH - 1)
                copy_out(KD)

            def mlp(last, next_layer):
                t0, n = tile[0], step[0]

                def block_of(f):
                    with dve.Fori(0, FB // 2) as i:
                        at = 2 * i + 2 * FB * f
                        m_at = i + FB // 2 * f
                        fa = hidden[0] + FB * f + 2 * i
                        for j in range(2):
                            if j == 0 and not last:
                                mod_copy(n, m_at)
                            if j == 1 and not last:
                                mod_add(next_layer, n, MU * m_at, m_at)
                            dve.wait_ge(relu_ready, fa + j + 1)
                            square = (ta, tb)[j]
                            dve.tensor_tensor(square[:, :], relu[:, j, :], relu[:, j, :], ALU.mult).then_inc(tile_read, 1)
                            dve.drain()
                            dve.wait_ge(fhi_ready, fa + j + 1)
                            dve.tensor_tensor(fs[:, 2 * i + j, 1, :], square[:, :], fs[:, 2 * i + j, 0, :].bitcast(F32),
                                              ALU.subtract).then_inc(f_ready, 1)
                    with dve.Fori(0, KD // 2) as i:
                        for j in range(2):
                            at = t0 + FB + j + 2 * i + 2 * FB * f
                            dve.wait_ge(tile_done, at + 1)
                            out = halves(acc[:, 2 * i + j, :])
                            if isinstance(f, int):
                                op = dve.tensor_copy(out, pu[:, (t0 + j) % 2, :, 0:HT])
                            else:
                                op = dve.tensor_tensor(out, pu[:, (t0 + j) % 2, :, 0:HT], out, ALU.add)
                            op.then_inc(tile_read, 1)

                block_of(0)
                with dve.Fori(1, NFB) as f:
                    block_of(f)
                tile[0] += MLP_SLABS
                hidden[0] += NFB * FB
                if not last:
                    step[0] += MSTEPS

            dve.memset(eps[:, :], EPS).then_inc(eps_made, 1)
            dve.memset(cs[:, :, :], 0.0)
            dve.drain()
            dve.wait_ge(gate_ready, 1)
            dve.tensor_scalar(cgate[:, :, :], cgate[:, :, :], 0.5, 0.5, ALU.mult, ALU.add)
            dve.drain()
            dve.tensor_tensor(cs[:, :, 0:2], cgate[:, :, :], cvec[:, :, :], ALU.mult).then_inc(cs_ready, 1)
            mod_copy(0)
            mod_add(layers[0], 0, 0)
            with dve.Fori(1, MSTEPS) as i:
                mod_copy(0, i)
                mod_add(layers[0], 0, MU * i, i)
            step[0] = MSTEPS
            coefficients(layers[0])
            for li, l in enumerate(layers):
                last = li == len(layers) - 1
                if l == 0:
                    modulate(0, 1, True)
                    fourier()
                if l == 1:
                    modulate(0, 1, False)
                    short_conv()
                if l == 2:
                    modulate(0, 1, True)
                    rwkv()
                if l == 3:
                    modulate(0, 1, False)
                    latent_attention()
                add_normed(2)
                modulate(3, 4, False)
                mlp(last, None if last else layers[li + 1])
                add_normed(5)
                if not last:
                    coefficients(layers[li + 1])


def slabs(w, kd=KD):
    k, m = w.shape
    return w.reshape(k // P, P, m // P, P).transpose(2, 1, 0, 3).reshape(m // P, P, k)


def feature_major(v):
    v = v.reshape(v.shape[:-1] + (v.shape[-1] // P, P))
    return np.moveaxis(v, -1, 0)


def dft(n, scale):
    angle = 2 * np.pi * (np.outer(np.arange(n), np.arange(n)) % n) / n
    return np.cos(angle) * scale, np.sin(angle) * scale


def constants():
    sel = np.zeros((P, 2))
    for g in range(4):
        sel[32 * g, 0] = sel[32 * g + 1, 1] = 1
    c, s = dft(P, 1.0)
    cos, sin, swap = rotary_tables()
    lat = dft(LAT, (LAT * P) ** -0.5)
    con = dft(CTX, (CTX * P) ** -0.5)
    n = np.arange(P)
    s_, t_ = n[:, None], n[None, :]
    mask = np.concatenate([t_ // 32 < s_ // 32, s_ < t_, s_ <= t_, s_ <= t_], 1).astype(np.uint32)
    out = {
        "wmask": np.tile(np.arange(T) % W != 0, (P, 1)), "blk": s_ // HS == t_ // HS,
        "cos": cos, "sin": sin, "swap": swap,
        "ones": np.ones((P, P)), "ident": np.eye(P), "sel": sel,
        "dfeat": np.concatenate([c, s], 1),
        "dlat": np.stack([m.reshape(LAT // P, P, LAT).transpose(1, 0, 2) for m in (lat[0], -lat[1])], 1),
        "dctx": np.stack([con[0], -con[1]], 1),
    }
    return {k: np.ascontiguousarray(v, dtype=np.float32) for k, v in out.items()} | {"mask": mask}


def mla_slabs(i):
    def pad(w):
        return np.pad(w, ((0, 0), (0, 0), (0, D - w.shape[2])))
    dkv = i["mla_w_dkv"][0]
    rope = dkv[:, KVR:]
    uq = i["mla_w_uq"][0].reshape(QR, MH, P + DR)
    uq = np.concatenate([uq[:, :, :P].reshape(QR, -1), uq[:, :, P:].reshape(QR, -1)], 1)
    uv = i["mla_w_uv"][0].reshape(NKV, P, 2, 512).transpose(2, 1, 0, 3).reshape(2, P, D)
    return [
        slabs(np.concatenate([i["mla_w_dq"][0], dkv[:, :KVR], rope, rope], 1)),
        pad(slabs(uq).reshape(6, 2, P, QR).transpose(0, 2, 1, 3).reshape(6, P, 2 * QR)),
        slabs(i["mla_w_uk"][0]).reshape(2, 4, P, KVR).transpose(0, 2, 1, 3).reshape(2, P, 4 * KVR),
        uv,
        slabs(i["mla_w_o"][0]),
    ]


def rotary_tables():
    quarter = DR // 4
    n = np.arange(LAT)
    pos = np.stack([n // GRID_W, n % GRID_W]).astype(np.float32)
    inv = np.float32(ROPE_BASE) ** (-np.arange(quarter, dtype=np.float32) / np.float32(quarter))
    angle = (pos[:, None, :] * inv[None, :, None]).astype(np.float32)
    c, s = np.cos(angle), np.sin(angle)
    cos = np.stack([c, c], 1).reshape(DR, LAT)
    sin = np.stack([-s, s], 1).reshape(DR, LAT)
    swap = np.zeros((P, P))
    for p in range(P):
        swap[p ^ quarter, p] = 1
    return np.concatenate([cos, cos]), np.concatenate([sin, sin]), swap


def lay_out(i, layers=(0, 1, 2, 3)):
    ws = []
    for l in layers:
        if l == 0:
            ws.append(slabs(i["fft_w_out"][0]))
        if l == 1:
            w = slabs(i["conv_w_in"][0])
            for m in range(KD):
                ws.append(w[[KD + m, 2 * KD + m, m]])
            ws.append(slabs(i["conv_w_out"][0]))
        if l == 3:
            ws += mla_slabs(i)
        if l == 2:
            ws.append(slabs(np.concatenate([*i["rwkv_w_l1"][0], *i["rwkv_a_l1"][0], i["rwkv_g_l1"][0]], 1)))
            ws += [slabs(i[f"rwkv_w_{c}"][0]) for c in "rkvo"]
        w1, w2 = slabs(i["mlp_w1"][l]), i["mlp_w2"][l]
        for f in range(NFB):
            ws.append(w1[f * FB:(f + 1) * FB])
            ws.append(slabs(w2[f * FB * P:(f + 1) * FB * P]))
    x = np.concatenate([i["x_sample"][0], i["x_prompt"][0]])
    return {
        "w_slabs": np.concatenate(ws),
        "m_slabs": np.concatenate([slabs(i["mod_w"][l]) for l in layers]),
        "x": np.ascontiguousarray(x.T).reshape(KD, P, T),
        "cvec": np.stack([i["c"][0], i["c_ctx"]]).reshape(2, KD, P).transpose(2, 1, 0),
        "modb": feature_major(i["mod_b"]),
        "ng": feature_major(i["norm_g"]),
        "mu": feature_major(i["rwkv_mu"][0]),
        "pv": feature_major(np.concatenate([i["rwkv_w0"][0], i["rwkv_a0"][0]] + [
            i[f"rwkv_{n}"][0].reshape(1, D) for n in ("k_k", "k_a", "r_k", "ln_g", "ln_b")])),
        "l2": np.stack([i["rwkv_w_l2"][0].reshape(P, D), i["rwkv_a_l2"][0].reshape(P, D), i["rwkv_g_l2"][0]]
                       ).reshape(3, P, KD, P).transpose(2, 1, 0, 3),
        "s0": i["state_rwkv"][0, 0].transpose(1, 3, 0, 2).reshape(KD, P, 2, HS),
        "gq": feature_major(i["mla_g_q"][0]),
        "gkv": feature_major(i["mla_g_kv"][0]),
        "kvc": i["cache_mla_ckv"][0, 0].T.reshape(NKV, P, PAST).transpose(1, 0, 2),
        "krc": i["cache_mla_krope"][0, 0].T,
        "cw": feature_major(i["conv_w"][0]),
    } | constants()


OUTPUTS = {"y": (KD, P, T), "ckv": (P, NKV, CTX), "kr": (DR, CTX), "state": (KD, P, 2, HS)}


def kernel(**inputs):
    import concourse.bacc as bacc
    from concourse.bass_utils import run_bass_kernel_spmd

    nc = bacc.Bacc("TRN2", target_bir_lowering=False, num_devices=1)
    arrays = {name: np.ascontiguousarray(v) for name, v in lay_out(inputs).items()}
    aps = {name: nc.dram_tensor(f"in_{name}", v.shape, mybir.dt.from_np(v.dtype), kind="ExternalInput").ap()
           for name, v in arrays.items()}
    for name, shape in OUTPUTS.items():
        aps[name] = nc.dram_tensor(f"out_{name}", shape, F32, kind="ExternalOutput").ap()
    build(nc, aps)
    r = run_bass_kernel_spmd(nc, [{f"in_{name}": v for name, v in arrays.items()}], core_ids=[0]).results[0]
    y = r["out_y"].reshape(D, T).T
    ckv = r["out_ckv"].transpose(2, 1, 0).reshape(1, 1, CTX, KVR)
    kr = r["out_kr"].T.reshape(1, 1, CTX, DR)
    state = r["out_state"].reshape(KD, 2, HS, 2, HS).transpose(3, 0, 1, 4, 2).reshape(1, 1, 2, NH, HS, HS)
    return (np.ascontiguousarray(y[LAT:])[None], np.ascontiguousarray(y[:LAT])[None], np.ascontiguousarray(state),
            np.ascontiguousarray(ckv), np.ascontiguousarray(kr))
```
